# Optimizing a Trainium2 kernel written in Bass

```python
import jax, jax.numpy as jnp
from jax import lax
import numpy as np

D_MODEL = 1024
BATCH = 1
SEQ = 512
DEPTH = 1

HEAD_DIM = 64
MOBA_HEADS = 8
MOBA_WIDTH = MOBA_HEADS * HEAD_DIM
MOBA_BLOCK = 256
MOBA_TOPK = 3
MOBA_Q_BLOCK = 64
ALIBI_MAX = 8.0
GLA_HEADS = 4
GLA_DK = 64
GLA_DV = 128
GLA_KEY_WIDTH = GLA_HEADS * GLA_DK
GLA_VAL_WIDTH = GLA_HEADS * GLA_DV
GLA_GATE_RANK = 16
GLA_GATE_TAU = 16.0
GLA_CHUNK = 64
MIX_WIDTH = MOBA_WIDTH + GLA_VAL_WIDTH
PROJ_WIDTH = 3 * MOBA_WIDTH + 2 * GLA_KEY_WIDTH + 2 * GLA_VAL_WIDTH + GLA_GATE_RANK
N_EXPERTS = 32
TOP_K = 4
D_EXPERT = D_MODEL
SWIGLU_ALPHA = 1.702
SWIGLU_LIMIT = 7.0
MOE_ROW_BLOCK = 128
PLE_DIM = 256
EPS = 1e-6

kernel_name = 'hybrid_moba_gla_moe_ple'

def rms_norm(x, g):
    xf = x.astype(jnp.float32)
    y = xf * lax.rsqrt(jnp.mean(xf * xf, axis=-1, keepdims=True) + EPS)
    return (y * g.astype(jnp.float32)).astype(x.dtype)

def moba_attention(q, k, v):
    B, H, S, Dh = q.shape
    f32 = jnp.float32
    nb = -(-S // MOBA_BLOCK)
    pad = nb * MOBA_BLOCK - S
    kb = jnp.pad(k, ((0, 0), (0, 0), (0, pad), (0, 0))).reshape(B, H, nb, MOBA_BLOCK, Dh)
    vb = jnp.pad(v, ((0, 0), (0, 0), (0, pad), (0, 0))).reshape(B, H, nb, MOBA_BLOCK, Dh)
    k_mean = jnp.mean(kb.astype(f32), axis=3)
    slopes = jnp.exp2(-ALIBI_MAX * jnp.arange(1, H + 1, dtype=f32) / H)[None, :, None, None]
    scale = Dh ** -0.5
    n_sel = min(MOBA_TOPK, nb - 1)
    nq = S // MOBA_Q_BLOCK
    q_blocks = q.reshape(B, H, nq, MOBA_Q_BLOCK, Dh).transpose(2, 0, 1, 3, 4)
    b_idx = jnp.arange(B)[:, None, None]
    h_idx = jnp.arange(H)[None, :, None]
    offs = jnp.arange(MOBA_BLOCK)

    def attend_block(args):
        qb, c = args
        qf = qb.astype(f32) * scale
        q_pos = c * MOBA_Q_BLOCK + jnp.arange(MOBA_Q_BLOCK)
        own = (c * MOBA_Q_BLOCK) // MOBA_BLOCK
        scores = []
        sel = None
        if n_sel > 0:
            gate = jnp.einsum('bhqd,bhnd->bhqn', qf, k_mean)
            gate = jnp.where(jnp.arange(nb) < own, gate, -jnp.inf)
            _, sel = lax.top_k(gate, n_sel)
            for j in range(n_sel):
                idx = sel[..., j]
                kj = kb[b_idx, h_idx, idx].astype(f32)
                s = jnp.einsum('bhqd,bhqkd->bhqk', qf, kj)
                dist = (q_pos[:, None] - (idx[..., None] * MOBA_BLOCK + offs)).astype(f32)
                s = jnp.where(j < own, s - slopes * dist, -jnp.inf)
                scores.append(s)
        ko = lax.dynamic_index_in_dim(kb, own, axis=2, keepdims=False).astype(f32)
        vo = lax.dynamic_index_in_dim(vb, own, axis=2, keepdims=False).astype(f32)
        dist = (q_pos[:, None] - (own * MOBA_BLOCK + offs)[None, :]).astype(f32)
        s = jnp.einsum('bhqd,bhkd->bhqk', qf, ko)
        s = jnp.where(dist >= 0, s - slopes * dist, -jnp.inf)
        scores.append(s)
        probs = jax.nn.softmax(jnp.concatenate(scores, axis=-1), axis=-1)
        probs = probs.reshape(B, H, MOBA_Q_BLOCK, n_sel + 1, MOBA_BLOCK)
        out = jnp.einsum('bhqk,bhkd->bhqd', probs[:, :, :, n_sel], vo)
        for j in range(n_sel):
            vj = vb[b_idx, h_idx, sel[..., j]].astype(f32)
            out = out + jnp.einsum('bhqk,bhqkd->bhqd', probs[:, :, :, j], vj)
        return out.astype(q.dtype)

    out = lax.map(attend_block, (q_blocks, jnp.arange(nq)))
    return out.transpose(1, 2, 0, 3, 4).reshape(B, H, S, Dh)

def gla_chunked(q, k, v, log_a):
    B, H, S, DK = q.shape
    DV = v.shape[-1]
    f32 = jnp.float32
    C = GLA_CHUNK
    nc = S // C
    qf = q.astype(f32).reshape(B, H, nc, C, DK) * DK ** -0.5
    kf = k.astype(f32).reshape(B, H, nc, C, DK)
    vf = v.astype(f32).reshape(B, H, nc, C, DV)
    G = jnp.cumsum(log_a.astype(f32).reshape(B, H, nc, C, DK), axis=3)
    G_last = G[:, :, :, -1:, :]
    q_dec = qf * jnp.exp(G)
    k_dec = kf * jnp.exp(-G)
    k_tail = kf * jnp.exp(G_last - G)
    causal = jnp.tril(jnp.ones((C, C), dtype=bool))
    A = jnp.where(causal, jnp.einsum('bhnqd,bhnkd->bhnqk', q_dec, k_dec), 0.0)
    o_intra = jnp.einsum('bhnqk,bhnkv->bhnqv', A, vf)
    kv = jnp.einsum('bhnkd,bhnkv->bhndv', k_tail, vf)
    decay = jnp.exp(G_last[:, :, :, 0, :])

    def step(state, inp):
        kv_c, d_c = inp
        return d_c[..., None] * state + kv_c, state

    _, s_prev = lax.scan(step, jnp.zeros((B, H, DK, DV), f32),
                         (kv.transpose(2, 0, 1, 3, 4), decay.transpose(2, 0, 1, 3)))
    s_prev = s_prev.transpose(1, 2, 0, 3, 4)
    o_inter = jnp.einsum('bhnqd,bhndv->bhnqv', q_dec, s_prev)
    return (o_intra + o_inter).reshape(B, H, S, DV).astype(v.dtype)

def clamped_swiglu(hid):
    x_glu = jnp.minimum(hid[..., ::2], SWIGLU_LIMIT)
    x_lin = jnp.clip(hid[..., 1::2], -SWIGLU_LIMIT, SWIGLU_LIMIT)
    return x_glu * jax.nn.sigmoid(SWIGLU_ALPHA * x_glu) * (x_lin + 1.0)

def moe_ffn(h, w_router, b_router, w1, b1, w2, b2):
    T, D = h.shape
    M = MOE_ROW_BLOCK
    logits = (h @ w_router + b_router).astype(jnp.float32)
    top_vals, top_idx = lax.top_k(logits, TOP_K)
    gates = jax.nn.softmax(top_vals, axis=-1).astype(h.dtype)
    n_assign = T * TOP_K
    flat_e = top_idx.reshape(-1)
    order = jnp.argsort(flat_e, stable=True)
    sorted_e = flat_e[order]
    sorted_tok = order // TOP_K
    sorted_gate = gates.reshape(-1)[order]
    counts = jnp.bincount(flat_e, length=N_EXPERTS)
    padded = (counts + M - 1) // M * M
    grp_start = jnp.cumsum(counts) - counts
    pad_end = jnp.cumsum(padded)
    pad_start = pad_end - padded
    dest = pad_start[sorted_e] + jnp.arange(n_assign) - grp_start[sorted_e]
    n_blocks = -(-n_assign // M) + N_EXPERTS
    n_rows = n_blocks * M
    row_tok = jnp.zeros((n_rows,), jnp.int32).at[dest].set(sorted_tok.astype(jnp.int32))
    row_gate = jnp.zeros((n_rows,), h.dtype).at[dest].set(sorted_gate)
    block_expert = jnp.minimum(jnp.searchsorted(pad_end, jnp.arange(n_blocks) * M, side='right'),
                               N_EXPERTS - 1)
    x_rows = h[row_tok].reshape(n_blocks, M, D)

    def expert_block(args):
        xb, e = args
        hid = xb @ w1[e] + b1[e]
        return clamped_swiglu(hid) @ w2[e] + b2[e]

    y = lax.map(expert_block, (x_rows, block_expert)).reshape(n_rows, D)
    return jnp.zeros_like(h).at[row_tok].add(y * row_gate[:, None])

def setup_inputs(seed: int = 0) -> dict:
    key = jax.random.key(seed)
    ks = jax.random.split(key, 19)
    L = DEPTH

    def nrm(k, shape, scale):
        return jax.random.normal(k, shape, jnp.float32) * scale

    return {
        'x': nrm(ks[0], (BATCH, SEQ, D_MODEL), 1.0),
        'p': nrm(ks[1], (DEPTH, BATCH, SEQ, PLE_DIM), 1.0),
        'g_mix': 1.0 + nrm(ks[2], (L, D_MODEL), 0.01),
        'w_in': nrm(ks[3], (L, D_MODEL, PROJ_WIDTH), D_MODEL ** -0.5),
        'w_gla_gate': nrm(ks[4], (L, GLA_GATE_RANK, GLA_KEY_WIDTH), GLA_GATE_RANK ** -0.5),
        'b_gla_gate': nrm(ks[5], (L, GLA_KEY_WIDTH), 0.1),
        'g_gla_norm': 1.0 + nrm(ks[6], (L, GLA_DV), 0.01),
        'w_out': nrm(ks[7], (L, MIX_WIDTH, D_MODEL), MIX_WIDTH ** -0.5),
        'g_ffn': 1.0 + nrm(ks[8], (L, D_MODEL), 0.01),
        'w_router': nrm(ks[9], (L, D_MODEL, N_EXPERTS), D_MODEL ** -0.5),
        'b_router': nrm(ks[10], (L, N_EXPERTS), 0.01),
        'w1': nrm(ks[11], (L, N_EXPERTS, D_MODEL, 2 * D_EXPERT), D_MODEL ** -0.5),
        'b1': nrm(ks[12], (L, N_EXPERTS, 2 * D_EXPERT), 0.01),
        'w2': nrm(ks[13], (L, N_EXPERTS, D_EXPERT, D_MODEL), D_EXPERT ** -0.5),
        'b2': nrm(ks[14], (L, N_EXPERTS, D_MODEL), 0.01),
        'w_ple_gate': nrm(ks[15], (L, D_MODEL, D_MODEL), D_MODEL ** -0.5),
        'w_ple_proj': nrm(ks[16], (L, PLE_DIM, D_MODEL), PLE_DIM ** -0.5),
        'g_ple': 1.0 + nrm(ks[17], (L, D_MODEL), 0.01),
        'g_final': 1.0 + nrm(ks[18], (D_MODEL,), 0.01),
    }

def reference(x, p, g_mix, w_in, w_gla_gate, b_gla_gate, g_gla_norm, w_out, g_ffn,
              w_router, b_router, w1, b1, w2, b2, w_ple_gate, w_ple_proj, g_ple, g_final):
    B, S, D = x.shape
    splits = list(np.cumsum([MOBA_WIDTH, MOBA_WIDTH, MOBA_WIDTH, GLA_KEY_WIDTH, GLA_KEY_WIDTH,
                             GLA_VAL_WIDTH, GLA_VAL_WIDTH])[:])
    splits = [int(s) for s in splits]
    h = x
    for i in range(DEPTH):
        a = rms_norm(h, g_mix[i])
        proj = a @ w_in[i]
        qa, ka, va, qg, kg, vg, rg, ag = jnp.split(proj, splits, axis=-1)
        to_heads = lambda t, nh: t.reshape(B, S, nh, -1).transpose(0, 2, 1, 3)
        o_moba = moba_attention(to_heads(qa, MOBA_HEADS), to_heads(ka, MOBA_HEADS),
                                to_heads(va, MOBA_HEADS))
        o_moba = o_moba.transpose(0, 2, 1, 3).reshape(B, S, MOBA_WIDTH)
        log_a = jax.nn.log_sigmoid((ag @ w_gla_gate[i] + b_gla_gate[i]).astype(jnp.float32)) / GLA_GATE_TAU
        o_gla = gla_chunked(to_heads(qg, GLA_HEADS), to_heads(kg, GLA_HEADS),
                            to_heads(vg, GLA_HEADS), to_heads(log_a, GLA_HEADS))
        o_gla = rms_norm(o_gla, g_gla_norm[i]).transpose(0, 2, 1, 3).reshape(B, S, GLA_VAL_WIDTH)
        o_gla = o_gla * jax.nn.silu(rg)
        h = h + jnp.concatenate([o_moba, o_gla], axis=-1) @ w_out[i]
        f = rms_norm(h, g_ffn[i]).reshape(B * S, D)
        h = h + moe_ffn(f, w_router[i], b_router[i], w1[i], b1[i], w2[i], b2[i]).reshape(B, S, D)
        ple = rms_norm(p[i] @ w_ple_proj[i], g_ple[i])
        h = h + jax.nn.sigmoid(h @ w_ple_gate[i]) * ple
    return rms_norm(h, g_final)


_drawn_inputs = setup_inputs


def setup_inputs(seed=0):
    import zlib

    import numpy as np

    out = dict(_drawn_inputs(seed))
    spreads = {}
    factors = {'g_gla_norm': 12.562,
     'b1': 25.215,
     'b2': 96.544,
     'g_ple': 200.0,
     'g_final': 199.029,
     'g_mix': 2.981,
     'g_ffn': 11.529,
     'b_router': 13.264}
    for name, (base, spread) in spreads.items():
        noise = np.random.default_rng([zlib.crc32(name.encode()), seed]).standard_normal(out[name].shape)
        drawn = base * np.exp(spread * noise) if base else spread * noise
        out[name] = __import__('jax').numpy.asarray(drawn.astype(out[name].dtype))
    for name, factor in factors.items():
        out[name] = (out[name] * factor).astype(out[name].dtype)
    return out
```

```python
from contextlib import ExitStack

import concourse.bass as bass
from concourse import mybir

F32 = mybir.dt.float32
I32 = mybir.dt.int32
U32 = mybir.dt.uint32
U8 = mybir.dt.uint8
ALU = mybir.AluOpType
ACT = mybir.ActivationFunctionType
AX = mybir.AxisListType

P = 128
SEQ = 512
D = 1024
NT = SEQ // P
NC = D // P
HD = 64
MH = 8
GH = 4
GC = 64
RANK = 16
TAU = 16.0
NE = 32
TOPK = 4
CAP = 96
NEXTRA = SEQ * TOPK // CAP
NBLK = NE + NEXTRA
NTAB = NBLK + 1
MAXFULL = (SEQ - 1) // CAP
LIMIT = 7.0
ALPHA = 1.702
EPS = 1e-6
MASKED = -1.0e30
WU = 6
SWI = 8
PLE = 256


def hybrid_layer(nc, x, p, g_mix, w_in, w_gla_gate, b_gla_gate, g_gla_norm, w_out, g_ffn, w_router, b_router,
                 w1, b1, w2, b2, w_ple_gate, w_ple_proj, g_ple, g_final, out):
    ctx = ExitStack()
    with ctx:
        def sb(name, shape, dt=F32):
            return ctx.enter_context(nc.sbuf_tensor(name, shape, dt))

        def sem(name):
            return ctx.enter_context(nc.semaphore(name))

        f_rows = nc.dram_tensor("f_rows", (SEQ, D), F32, kind="Internal").ap()
        y_rows = nc.dram_tensor("y_rows", (NBLK * CAP, D), F32, kind="Internal").ap()
        ple_rows = nc.dram_tensor("ple_rows", (SEQ, D), F32, kind="Internal").ap()

        W = sb("W", [P, 24576])
        w1q = W[:, 0:16384].rearrange("p (q c n) -> p q c n", q=4, c=NC)
        w2h = W[:, 16384:24576].rearrange("p (f n) -> p f n", f=NC)

        def in_w(at, *shape):
            n = 1
            for s in shape:
                n *= s
            v = W[:, at:at + n]
            return v.rearrange("p (a b) -> p a b", a=shape[0]) if len(shape) == 2 else v

        aT = in_w(0, NC, SEQ)
        qT = in_w(4096, 4, SEQ)
        kT = in_w(6144, 4, SEQ)
        xs = in_w(4096, NT, D)
        v_ = in_w(8192, NT, 512)
        vg = in_w(10240, NT, 512)
        rg = in_w(12288, NT, 512)
        b1raw = W[0:NE, 12288:14336]
        b2raw = W[0:NE, 14336:15360]
        qz = in_w(14336 + 1024, GH, SEQ)
        kd = in_w(17408, 2, SEQ)
        qraw = in_w(18432, 2, SEQ)
        kraw = in_w(19456, 2, SEQ)
        G = in_w(20480, 2, SEQ)
        eG = in_w(21504, 2, SEQ)
        tmpG = in_w(22528, 2, SEQ)
        ktok = in_w(23552, NT, 256)
        ktail = in_w(14336, 2, SEQ)
        yg = in_w(0, 16, D)
        ple_in = in_w(16384, NT, D)
        gfin = W[:, 20480:21504]

        H = sb("H", [P, NT, D])
        actT = sb("actT", [P, NC, SEQ])
        wst = sb("wst", [P, 2, NC, 512])
        wpp = wst[:, 0, 0:4, :].rearrange("p a b -> p (a b)").rearrange("p (c n) -> p c n", c=2)
        prow = wst[:, 0, 4:6, :].rearrange("p a b -> p (a b)").rearrange("p (t n) -> p t n", t=NT)
        pT = wst[:, 0, 6:8, :]
        pleo = wst[:, 1, :, :].rearrange("p a b -> p (a b)").rearrange("p (t n) -> p t n", t=NT)

        M = sb("M", [P, 7680])
        Pm = M[:, 0:2048].rearrange("p (b n) -> p b n", b=4)
        PTs = M[:, 2048:3072].rearrange("p (b n) -> p b n", b=2)
        AT = M[:, 3072:3584]
        OMS = M[:, 3584:4096]
        ON = M[:, 4096:4608]
        st = M[:, 4608:6656].rearrange("p (c h n) -> p c h n", c=8, h=2)
        F = M[:, 6656:7680]
        gple = M[:, 6656:7680]
        zero = M[0:CAP, 6656:7680]
        oh = M[:, 0:512].rearrange("p (a e) -> p a e", e=NE)
        prod = M[:, 512:1024].rearrange("p (a e) -> p a e", e=NE)
        ohJ = M[:, 1024:2560].rearrange("p (a j) -> p a j", j=CAP)
        ohB = M[:, 2560:2560 + 16 * NTAB].rearrange("p (a b) -> p a b", b=NTAB)
        XT = M[:, 3456:4224].rearrange("p (c j) -> p c j", c=NC)
        XG = M[0:CAP, 4608:5632]
        HID = M[:, 0:768].rearrange("p (f j) -> p f j", f=NC)
        T1 = M[:, 768:1152].rearrange("p (f j) -> p f j", f=4)
        T2 = M[:, 1152:1536].rearrange("p (f j) -> p f j", f=4)
        SIG = M[:, 1536:1920].rearrange("p (f j) -> p f j", f=4)
        YT = M[:, 1920:2688].rearrange("p (m j) -> p m j", m=NC)
        YR = M[0:CAP, 5632:6656]
        SG = M[:, 0:2048].rearrange("p (b n) -> p b n", b=2)
        OUTB = M[:, 2048:4096].rearrange("p (b n) -> p b n", b=2)

        ident = sb("ident", [P, P])
        before = sb("before", [P, P])
        ones = sb("ones", [P, P])
        chunk_ok = sb("chunk_ok", [P, GH, P], U8)
        keep = M[:, 128:640]
        dist = sb("dist", [P, 1280])
        it_j = sb("it_j", [P, CAP])
        it_b = sb("it_b", [P, NTAB])
        tok = sb("tok", [P, NT])
        mhalf = sb("mhalf", [P, 8])
        vraw = M[0:19, 0:P]
        vc = sb("vc", [P, 19])
        brow = sb("brow", [1, NE])
        wag = sb("wag", [P, NC, RANK])
        wgate = sb("wgate", [RANK, 256])
        wr = sb("wr", [P, NC, NE])
        agT = M[0:RANK, 2048:2560]
        b1T = sb("b1T", [P, NC, 2, NE])
        b2T = sb("b2T", [P, NC, NE])
        ss = sb("ss", [P, 8])
        rstd = sb("rstd", [P, 8])
        ssg = sb("ssg", [P, GH])
        rsg = sb("rsg", [P, GH])
        nmax = sb("nmax", [P, NT * MH])
        rsum = sb("rsum", [P, NT * MH])
        rinv = sb("rinv", [P, NT * MH])
        L = sb("L", [P, NT, NE])
        top8 = sb("top8", [P, NT, 8])
        idx8 = sb("idx8", [P, NT, 8], U32)
        idxf = sb("idxf", [P, NT, TOPK])
        ex4 = sb("ex4", [P, NT, TOPK])
        gate = sb("gate", [P, NT, TOPK])
        s4 = sb("s4", [P, NT])
        Mk = sb("Mk", [P, NT, NE])
        full, has, Jm = (M[:, a:a + NT * NE].rearrange("p (t e) -> p t e", t=NT) for a in (5376, 5504, 5632))
        cnt = sb("cnt", [P, NE])
        extra = sb("extra", [P, NE])
        xend = sb("xend", [P, NE])
        xbase = sb("xbase", [P, NE])
        Bs = sb("Bs", [P, NT * TOPK])
        Js = sb("Js", [P, NT * TOPK])
        slotf = sb("slotf", [P, NT * TOPK])
        sloti = sb("sloti", [P, NT * TOPK], I32)
        tokix = sb("tokix", [CAP, NTAB], I32)
        xcmp = M[0:1, 4608:4608 + NEXTRA * NE].rearrange("p (b e) -> p b e", b=NEXTRA)
        held = sb("held", [1, 1])
        tabf = sb("tabf", [1, NEXTRA + 1])
        tab = sb("tab", [1, NEXTRA + 1], I32)

        ps = ctx.enter_context(nc.psum_tensor("ps", [P, 8, 512], F32))

        x_in = [sem(f"x_in{t}") for t in range(NT)]
        vec_in = sem("vec_in")
        small_in = sem("small_in")
        bias_in = sem("bias_in")
        wst_in = [sem("wst_in0"), sem("wst_in1")]
        ple_ld = sem("ple_ld")
        gple_in = sem("gple_in")
        w_in_s = [sem(f"w_unit_in{u}") for u in range(WU)]
        w_used = sem("w_used")
        consts = sem("consts")
        pool_step = sem("pool_step")
        act_step = sem("act_step")
        dve_step = sem("dve_step")
        turned = sem("turned")
        turned_out = sem("turned_out")
        x_rstd = sem("x_rstd")
        ms_ready = sem("ms_ready")
        rstd_ready = sem("rstd_ready")
        xs_ready = sem("xs_ready")
        proj = sem("proj")
        proj_out = sem("proj_out")
        gx_ready = sem("gx_ready")
        gabs = sem("gabs")
        gln = sem("gln")
        g_ready = sem("g_ready")
        eg_ready = sem("eg_ready")
        eg_neg = sem("eg_neg")
        dg_ready = sem("dg_ready")
        dg_exp = sem("dg_exp")
        kt_ready = sem("kt_ready")
        gla_kq = sem("gla_kq")
        kv_done = sem("kv_done")
        st_ready = sem("st_ready")
        sig_r = sem("sig_r")
        rg_ready = sem("rg_ready")
        a_done = sem("a_done")
        a_out = sem("a_out")
        s_done = sem("s_done")
        s_masked = sem("s_masked")
        m_ready = sem("m_ready")
        p_exp = sem("p_exp")
        pt_done = sem("pt_done")
        pt_out = sem("pt_out")
        pv_done = sem("pv_done")
        om_out = sem("om_out")
        go_done = sem("go_done")
        go_sq = sem("go_sq")
        go_ss = sem("go_ss")
        go_rs = sem("go_rs")
        on_ready = sem("on_ready")
        tm_done = sem("tm_done")
        tm_out = sem("tm_out")
        tg_done = sem("tg_done")
        tg_out = sem("tg_out")
        wo_done = sem("wo_done")
        h_ready = sem("h_ready")
        h_ss = sem("h_ss")
        h_ms = sem("h_ms")
        h_rs = sem("h_rs")
        f_ready = sem("f_ready")
        f_stored = sem("f_stored")
        ft_done = sem("ft_done")
        ft_out = sem("ft_out")
        lg_done = sem("lg_done")
        lg_out = sem("lg_out")
        e_in = sem("e_in")
        e_out = sem("e_out")
        mk_ready = sem("mk_ready")
        rank_done = sem("rank_done")
        oh_ready = sem("oh_ready")
        tok_done = sem("tok_done")
        tab_ready = sem("tab_ready")
        slot_ready = sem("slot_ready")
        pt2_done = sem("pt2_done")
        pt2_out = sem("pt2_out")
        pp_done = sem("pp_done")
        pp_ss = sem("pp_ss")
        pp_ms = sem("pp_ms")
        pp_rs = sem("pp_rs")
        pp_out = sem("pp_out")
        ple_ready = sem("ple_ready")
        ple_stored = sem("ple_stored")
        blocks_done = sem("blocks_done")
        xg_in = sem("xg_in")
        zero_ready = sem("zero_ready")
        y_zeroed = sem("y_zeroed")
        xt_done = sem("xt_done")
        xt_ready = sem("xt_ready")
        moe_step = sem("moe_step")
        glu_min = sem("glu_min")
        sig_done = sem("sig_done")
        hid_done = sem("hid_done")
        yt_ready = sem("yt_ready")
        yr_done = sem("yr_done")
        yr_out = sem("yr_out")
        y_stored = sem("y_stored")
        yg_in = [sem(f"yg_in{t}") for t in range(NT)]
        tail_in = sem("tail_in")
        h2_ready = sem("h2_ready")
        h2t_done = sem("h2t_done")
        h2t_out = sem("h2t_out")
        gm_done = sem("gm_done")
        gm_sig = sem("gm_sig")
        h3_ready = sem("h3_ready")
        h3_ss = sem("h3_ss")
        h3_ms = sem("h3_ms")
        h3_rs = sem("h3_rs")
        o_ready = sem("o_ready")
        o_stored = [sem("o_stored0"), sem("o_stored1")]

        CH = [("qk_g", 1536), ("v_g", 2048), ("q", 0), ("k", 512), ("v", 1024), ("r", 2560)]
        w_in_v = w_in[0].rearrange("(c p) n -> p c n", p=P)

        GRP_AG = 8
        GRP_GATE = 9
        GRP = {"qk_g": 11, "v_g": 15, "q": 19, "k": 23, "ktok": 27, "v": 29, "r": 33}
        NGRP = 37
        slope = [2.0 ** (-8.0 * (h + 1) / MH) for h in range(MH)]
        dbase = [0, 128, 384, 768]

        def load_expert(sp, b, e, guard):
            for u in range(WU):
                if guard:
                    sp.wait_ge(w_used, b * WU + (u + 1 - WU))
                if u < 4:
                    src = w1[0, bass.ds(e, 1), :, u * 512:(u + 1) * 512].rearrange("o (c p) n -> p (o c) n", p=P)
                    sp.dma_start(w1q[:, u], src).then_inc(w_in_s[u], 16)
                else:
                    k = u - 4
                    src = w2[0, bass.ds(e, 1), k * 512:(k + 1) * 512, :].rearrange("o (c p) n -> p (o c) n", p=P)
                    sp.dma_start(w2h[:, 4 * k:4 * k + 4], src).then_inc(w_in_s[u], 16)

        def extra_blocks(eng, body):
            n = eng.value_load(tab[0:1, NEXTRA:NEXTRA + 1], min_val=0, max_val=NEXTRA)
            with eng.If(n > 0):
                with eng.Fori(0, n) as i:
                    body(i)
            return n

        block = ctx.enter_context(nc.Block())

        @block.sync
        def _(sp):
            for t in range(NT):
                sp.dma_start(H[:, t], x[0, t * P:(t + 1) * P, :]).then_inc(x_in[t], 16)
            sp.dma_start(vraw[0:8, :], g_mix[0].rearrange("(c p) -> c p", p=P)).then_inc(vec_in, 16)
            sp.dma_start(vraw[8:16, :], g_ffn[0].rearrange("(c p) -> c p", p=P)).then_inc(vec_in, 16)
            sp.dma_start(vraw[16:18, :], b_gla_gate[0].rearrange("(c p) -> c p", p=P)).then_inc(vec_in, 16)
            sp.dma_start(vraw[18:19, :], g_gla_norm).then_inc(vec_in, 16)
            sp.dma_start(wag[:], w_in_v[:, :, 3072:3088]).then_inc(vec_in, 16)
            for i in range(2):
                sp.dma_start(wst[:, i], w_in_v[:, :, CH[i][1]:CH[i][1] + 512]).then_inc(wst_in[i], 16)
            sp.dma_start(b1raw, b1[0]).then_inc(bias_in, 16)
            sp.dma_start(b2raw, b2[0]).then_inc(bias_in, 16)
            for i in range(2, 6):
                sp.wait_ge(proj, GRP[CH[i - 2][0]] + 4)
                sp.dma_start(wst[:, i % 2], w_in_v[:, :, CH[i][1]:CH[i][1] + 512]).then_inc(wst_in[i % 2], 16)
            sp.wait_ge(zero_ready, 1)
            sp.dma_start(y_rows[NE * CAP:, :].rearrange("(i r) n -> r i n", r=CAP), zero.unsqueeze(1).to_broadcast([CAP, NEXTRA, D])).then_inc(y_zeroed, 16)
            wo_v = w_out[0].rearrange("(c p) n -> p c n", p=P)
            for n in range(2):
                sp.wait_ge(proj, GRP[CH[4 + n][0]] + 4)
                sp.dma_start(wst[:, n], wo_v[:, :, n * 512:(n + 1) * 512]).then_inc(wst_in[n], 16)
            sp.wait_ge(tg_done, NT)
            sp.wait_ge(on_ready, NT)
            load_expert(sp, 0, 0, False)
            sp.wait_ge(ple_ready, NT)
            for t in range(NT):
                sp.dma_start(ple_rows[t * P:(t + 1) * P, :], pleo[:, t]).then_inc(ple_stored, 16)
            sp.wait_ge(ple_stored, 16 * NT)
            wg_v = w_ple_gate[0].rearrange("(c p) n -> p c n", p=P)
            for n in range(2):
                sp.dma_start(wst[:, n], wg_v[:, :, n * 512:(n + 1) * 512]).then_inc(wst_in[n], 16)
            with sp.Fori(1, NE) as b:
                load_expert(sp, b, b, True)
            sp.wait_ge(tab_ready, 1)

            def body(i):
                e = sp.value_load(tab[0:1, bass.ds(i, 1)], min_val=0, max_val=NE - 1)
                load_expert(sp, i + NE, e, True)
            n = extra_blocks(sp, body)
            sp.wait_ge(w_used, (n + NE) * WU)
            sp.dma_start(ple_in, ple_rows.rearrange("(t p) n -> p t n", p=P)).then_inc(tail_in, 16)
            sp.dma_start(gfin, g_final.partition_broadcast(P)).then_inc(tail_in, 16)
            for t in range(NT):
                sp.wait_ge(o_ready, t + 1)
                sp.dma_start(out[0, t * P:(t + 1) * P, :], OUTB[:, t % 2]).then_inc(o_stored[t % 2], 16)
            for i in range(2):
                sp.wait_ge(o_stored[i], 16 * (NT // 2))

        @block.gpsimd
        def _(pool):
            made = [0]

            def link(ins):
                made[0] += 1
                ins.then_inc(pool_step, 1)
                pool.wait_ge(pool_step, made[0])

            consts_made = [0]

            def const(ins):
                consts_made[0] += 1
                ins.then_inc(consts, 1)
                pool.wait_ge(consts, consts_made[0])

            pool.dma_start(wgate[:], w_gla_gate[0]).then_inc(small_in, 16)
            pool.dma_start(wr[:], w_router[0].rearrange("(c p) n -> p c n", p=P)).then_inc(small_in, 16)
            pool.dma_start(brow[:], b_router).then_inc(small_in, 16)
            link(pool.memset(ident[:], 0.0))
            const(pool.affine_select(out=ident[:], in_=ident[:], compare_op=ALU.not_equal, fill=1.0, base=0,
                               pattern=[[-1, P]], channel_multiplier=1))
            const(pool.memset(mhalf[:], -0.5))
            link(pool.memset(ones[:], 1.0))
            const(pool.affine_select(out=before[:], in_=ones[:], compare_op=ALU.is_gt, fill=0.0, base=0,
                               pattern=[[1, P]], channel_multiplier=-1))
            link(pool.memset(keep, 1.0))
            const(pool.memset(keep[:, 0:SEQ:GC], 0.0))
            link(pool.iota(dist[:, 0:512], [[0, GH], [1, P]], base=1, channel_multiplier=-1, allow_small_or_imprecise_dtypes=True))
            link(pool.tensor_scalar(dist[:, 0:512], dist[:, 0:512], 0.0, None, ALU.max))
            link(pool.tensor_scalar(dist[:, 0:512], dist[:, 0:512], 1.0, None, ALU.min))
            for h in range(GH):
                link(pool.memset(dist[0:GC, h * P + GC:(h + 1) * P], 0.0))
            link(pool.tensor_copy(chunk_ok[:], dist[:, 0:512].rearrange("p (h q) -> p h q", h=GH)))
            for t in range(NT):
                n = (t + 1) * P
                dt_ = dist[:, dbase[t]:dbase[t] + n]
                link(pool.iota(dt_, [[1, n]], base=-t * P, channel_multiplier=-1, allow_small_or_imprecise_dtypes=True))
                const(pool.affine_select(out=dt_, in_=dt_, compare_op=ALU.is_ge, fill=MASKED * 256.0, base=t * P,
                                   pattern=[[-1, n]], channel_multiplier=1))
            const(pool.iota(it_j[:], [[1, CAP]], base=0, channel_multiplier=0, allow_small_or_imprecise_dtypes=True))
            const(pool.iota(it_b[:], [[1, NTAB]], base=0, channel_multiplier=0, allow_small_or_imprecise_dtypes=True))
            const(pool.iota(tok[:], [[P, NT]], base=0, channel_multiplier=1, allow_small_or_imprecise_dtypes=True))
            pool.wait_ge(consts, 2)
            pool.wait_ge(x_rstd, 1)
            pool.tensor_tensor(rstd[:, 0:NT], ss[:, 0:NT], mhalf[:, 0:NT], ALU.pow).then_inc(rstd_ready, 1)
            pool.wait_ge(turned_out, 2)
            for h in range(GH):
                lo = 64 * (1 - h % 2)
                const(pool.memset(qz[lo:lo + 64, h, :], 0.0))
            const(pool.memset(st[:, 0], 0.0))
            const(pool.memset(AT, 0.0))
            pool.memset(zero, 0.0).then_inc(zero_ready, 1)

            def go_rstd(t):
                pool.wait_ge(go_ss, t + 1)
                pool.tensor_tensor(rsg[:], ssg[:], mhalf[:, 0:GH], ALU.pow).then_inc(go_rs, 1)

            def h_rstd(t):
                pool.wait_ge(h_ms, t + 1)
                pool.tensor_tensor(rstd[:, 4:5], ss[:, 4:5], mhalf[:, 0:1], ALU.pow).then_inc(h_rs, 1)

            for t in range(NT):
                if t > 0:
                    h_rstd(t - 1)
                go_rstd(t)
            h_rstd(NT - 1)
            pool.wait_ge(f_stored, 16 * NT)
            pool.wait_ge(ft_done, 2 * NT)
            pool.dma_start(gple, g_ple[0].partition_broadcast(P)).then_inc(gple_in, 16)
            for t in range(NT):
                pool.wait_ge(pp_ss, t + 1)
                link(pool.tensor_scalar(ss[:, 5:6], ss[:, 7:8], 1.0 / D, EPS, ALU.mult, ALU.add))
                pool.tensor_tensor(rstd[:, 5:6], ss[:, 5:6], mhalf[:, 0:1], ALU.pow).then_inc(pp_rs, 1)
                pool.wait_ge(pp_out, t + 1)
                if t == 0:
                    pool.wait_ge(gple_in, 16)
                pool.tensor_tensor(pleo[:, t], pleo[:, t], gple, ALU.mult).then_inc(ple_ready, 1)

            def gather(b):
                if b > 0:
                    pool.wait_ge(xt_done, b)
                pool.indirect_dma_start(XG, None, f_rows, bass.IndirectOffsetOnAxis(ap=tokix[:, b:b + 1].bitcast(U32), axis=0)).then_inc(xg_in, 16)

            pool.wait_ge(tab_ready, 1)
            for b in range(NE + 1):
                gather(b)
            n = pool.value_load(tab[0:1, NEXTRA:NEXTRA + 1], min_val=0, max_val=NEXTRA)
            for i in range(NEXTRA):
                with pool.If(n > i):
                    gather(NE + 1 + i)
            pool.wait_ge(blocks_done, 1)
            for t in range(NT):
                for k in range(TOPK):
                    s = t * TOPK + k
                    pool.indirect_dma_start(yg[:, s], None, y_rows, bass.IndirectOffsetOnAxis(ap=sloti[:, s:s + 1].bitcast(U32), axis=0)).then_inc(yg_in[t], 16)
            for t in range(NT):
                pool.wait_ge(h3_ms, t + 1)
                pool.tensor_tensor(rstd[:, 6:7], ss[:, 6:7], mhalf[:, 0:1], ALU.pow).then_inc(h3_rs, 1)

        @block.scalar
        def _(act):
            for t in range(NT):
                act.wait_ge(x_in[t], 16)
                act.activation(xs[:, t], H[:, t], ACT.Square, accum_out=ss[:, t:t + 1]).then_inc(ms_ready, 1)

            act.wait_ge(turned_out, 1)
            for g in range(NC):
                act.wait_ge(proj, g + 1)
                act.activation(aT[:, g], ps[:, g % 4], ACT.Copy, scale=vc[:, g:g + 1]).then_inc(proj_out, 1)

            def evac(g, dst, scale=1.0):
                act.wait_ge(proj, g + 1)
                act.activation(dst, ps[0:dst.shape[0], g % 4], ACT.Copy, scale=scale).then_inc(proj_out, 1)

            evac(GRP_AG, agT)
            for hp in range(2):
                act.wait_ge(proj, GRP_GATE + hp + 1)
                act.activation(G[:, hp], ps[:, (GRP_GATE + hp) % 4], ACT.Identity, bias=vc[:, 16 + hp:17 + hp]).then_inc(proj_out, 1)
            act.wait_ge(proj_out, GRP_GATE + 2)
            act.activation(tmpG, G, ACT.Abs).then_inc(gx_ready, 1)
            act.wait_ge(gx_ready, 1)
            act.activation(tmpG, tmpG, ACT.Exp, scale=-1.0).then_inc(gabs, 1)
            act.wait_ge(gabs, 1)
            act.activation(tmpG, tmpG, ACT.Ln, bias=1.0).then_inc(gln, 1)
            for i in range(4):
                dst = qraw[:, i] if i < 2 else kraw[:, i - 2]
                evac(GRP["qk_g"] + i, dst, HD ** -0.5 if i < 2 else 1.0)
            act.wait_ge(g_ready, 2)
            act.activation(eG, G, ACT.Exp, scale=1.0 / TAU).then_inc(eg_ready, 1)
            act.activation(tmpG, G, ACT.Exp, scale=-1.0 / TAU).then_inc(eg_neg, 1)
            for t in range(NT):
                evac(GRP["v_g"] + t, vg[:, t])
            act.wait_ge(dg_ready, 2)
            act.activation(ktail, ktail, ACT.Exp, scale=1.0 / TAU).then_inc(dg_exp, 1)
            for i in range(4):
                evac(GRP["q"] + i, qT[:, i], HD ** -0.5)
            for i in range(4):
                evac(GRP["k"] + i, kT[:, i])
            for hp in range(2):
                act.wait_ge(proj, GRP["ktok"] + hp + 1)
                act.activation(ktok[:, :, hp * P:(hp + 1) * P], ps[:, (GRP["ktok"] + hp) % 4].rearrange("p (t f) -> p t f", t=NT),
                               ACT.Copy).then_inc(proj_out, 1)
            for t in range(NT):
                evac(GRP["v"] + t, v_[:, t])
            for t in range(NT):
                g = GRP["r"] + t
                act.wait_ge(proj, g + 1)
                if t >= 1:
                    act.wait_ge(rg_ready, t)
                else:
                    act.wait_ge(gla_kq, 6)
                act.activation(rg[:, t], ps[:, g % 4], ACT.Copy).then_inc(sig_r, 1)
                act.activation(tmpG[:, 0], ps[:, g % 4], ACT.Sigmoid).then_inc(proj_out, 1)

            def expo(u):
                act.wait_ge(m_ready, u + 1)
                n = (u // MH + 1) * P
                act.activation(Pm[:, u % 4, 0:n], Pm[:, u % 4, 0:n], ACT.Exp, bias=nmax[:, u:u + 1],
                               accum_out=rsum[:, u:u + 1]).then_inc(p_exp, 1)

            def pt_copy(u):
                act.wait_ge(pt_done, u + 1)
                if u >= 2:
                    act.wait_ge(pv_done, u - 1)
                n = (u // MH + 1) * P
                act.activation(PTs[:, u % 2, 0:n], ps[:, 6 + u % 2, 0:n], ACT.Copy).then_inc(pt_out, 1)

            def h_square(t):
                act.wait_ge(h_ready, 2 * t + 2)
                if t == 0:
                    act.wait_ge(y_zeroed, 16)
                else:
                    act.wait_ge(f_stored, 16 * t)
                    act.wait_ge(ft_done, 2 * t)
                act.activation(F, H[:, t], ACT.Square, accum_out=ss[:, 4:5]).then_inc(h_ss, 1)

            def store_f(t):
                act.wait_ge(f_ready, t + 1)
                act.dma_start(f_rows[t * P:(t + 1) * P, :], F).then_inc(f_stored, 16)

            for t in range(NT):
                for i in range(MH + 1):
                    if i < MH:
                        expo(t * MH + i)
                    if i >= 1:
                        pt_copy(t * MH + i - 1)
                if t >= 1:
                    h_square(t - 1)
                act.wait_ge(go_done, t + 1)
                if t >= 1:
                    act.wait_ge(tg_done, t)
                act.activation(ON, ps[:, 1], ACT.Square).then_inc(go_sq, 1)
                act.wait_ge(tm_done, t + 1)
                act.activation(actT[:, 0:4, t * P:(t + 1) * P], ps[:, 2].rearrange("p (c q) -> p c q", c=4), ACT.Copy).then_inc(tm_out, 1)
                if t >= 1:
                    store_f(t - 1)
                act.wait_ge(tg_done, t + 1)
                act.activation(actT[:, 4:8, t * P:(t + 1) * P], ps[:, 2].rearrange("p (c q) -> p c q", c=4), ACT.Copy,
                               scale=vc[:, 18:19]).then_inc(tg_out, 1)
            h_square(NT - 1)
            store_f(NT - 1)
            act.wait_ge(wo_done, 2 * NT)
            act.dma_start(wpp, w_ple_proj[0].rearrange("(c p) n -> p c n", p=P)).then_inc(ple_ld, 16)
            act.dma_start(prow, p[0, 0].rearrange("(t p) n -> p t n", p=P)).then_inc(ple_ld, 16)
            act.wait_ge(e_in, 1)
            act.activation(ex4[:], ex4[:], ACT.Exp).then_inc(e_out, 1)
            for c in range(2):
                act.wait_ge(pt2_done, c + 1)
                act.activation(pT[:, c], ps[:, 4 + c], ACT.Copy).then_inc(pt2_out, 1)
            for t in range(NT):
                a = 2 * (t % 2)
                pl = ps[:, a:a + 2].rearrange("p a n -> p (a n)")
                act.wait_ge(pp_done, t + 1)
                act.activation(pleo[:, t], pl, ACT.Square, accum_out=ss[:, 7:8]).then_inc(pp_ss, 1)
                act.wait_ge(pp_rs, t + 1)
                act.activation(pleo[:, t], pl, ACT.Copy, scale=rstd[:, 5:6]).then_inc(pp_out, 1)

            def sigmoid(b, hf):
                act.wait_ge(glu_min, b * 2 + (hf + 1))
                act.activation(SIG, T1, ACT.Sigmoid, scale=ALPHA).then_inc(sig_done, 1)

            def store_y(b):
                act.wait_ge(yr_done, b + 1)
                for i in range(2):
                    act.activation(YR[:, i * 512:(i + 1) * 512], ps[0:CAP, 6 + i], ACT.Copy).then_inc(yr_out, 1)
                act.wait_ge(yr_out, b * 2 + 2)
                act.dma_start(y_rows[bass.ds(b * CAP, CAP), :], YR).then_inc(y_stored, 16)

            sigmoid(0, 0)
            sigmoid(0, 1)

            def body(b):
                sigmoid(b, 0)
                store_y(b - 1)
                sigmoid(b, 1)
                act.wait_ge(y_stored, b * 16)
            with act.Fori(1, NE) as b:
                body(b)
            n = extra_blocks(act, lambda i: body(i + NE))
            store_y(n + (NE - 1))
            act.wait_ge(y_stored, (n + NE) * 16)
            act.activation(held[:], tok[0:1, 0:1], ACT.Copy).then_inc(blocks_done, 1)
            def tail_norm(t):
                act.wait_ge(h3_ready, t + 1)
                if t >= 2:
                    act.wait_ge(o_stored[t % 2], 16 * (t // 2))
                act.activation(OUTB[:, t % 2], H[:, t], ACT.Square, accum_out=ssg[:, t:t + 1]).then_inc(h3_ss, 1)

            for t in range(NT):
                for i in range(2):
                    act.wait_ge(h2t_done, 2 * t + i + 1)
                    act.activation(actT[:, 4 * i:4 * i + 4, t * P:(t + 1) * P], ps[:, i].rearrange("p (c q) -> p c q", c=4),
                                   ACT.Copy).then_inc(h2t_out, 1)
                if t >= 1:
                    tail_norm(t - 1)
                act.wait_ge(gm_done, t + 1)
                if t >= 2:
                    act.wait_ge(h3_ready, t - 1)
                a = 2 + 2 * (t % 2)
                act.activation(SG[:, t % 2], ps[:, a:a + 2].rearrange("p a n -> p (a n)"), ACT.Sigmoid).then_inc(gm_sig, 1)
            tail_norm(NT - 1)

        @block.tensor
        def _(pe):
            pe.wait_ge(consts, 1)
            pe.wait_ge(vec_in, 80)
            pe.transpose(ps[:, 7, 0:19], vraw, ident[0:19, 0:19]).then_inc(turned, 1)
            for c in range(NC):
                if c >= 4:
                    pe.wait_ge(proj_out, c - 3)
                for t in range(NT):
                    if c == 0:
                        pe.wait_ge(xs_ready, t + 1)
                    last = pe.transpose(ps[:, c % 4, t * P:(t + 1) * P], xs[:, t, c * P:(c + 1) * P], ident[:])
                last.then_inc(proj, 1)
            pe.wait_ge(bias_in, 32)
            for c in range(NC):
                for s in range(2):
                    at = (c * 2 + s) * NE
                    last = pe.transpose(ps[:, 5, at:at + NE], b1raw[:, 2 * c * P + s:2 * (c + 1) * P:2], ident[0:NE, 0:NE])
            for c in range(NC):
                last = pe.transpose(ps[:, 6, c * NE:(c + 1) * NE], b2raw[:, c * P:(c + 1) * P], ident[0:NE, 0:NE])
            last.then_inc(turned, 1)

            def group(g, dst, pairs, inc=proj):
                pe.wait_ge(proj_out, g - 3)
                for i, (l, r) in enumerate(pairs):
                    last = pe.matmul(dst, l, r, start=(i == 0), stop=(i == len(pairs) - 1))
                last.then_inc(inc, 1)

            pe.wait_ge(small_in, 48)
            pe.wait_ge(proj_out, NC)
            group(GRP_AG, ps[0:RANK, GRP_AG % 4], [(wag[:, c, :], aT[:, c]) for c in range(NC)])
            pe.wait_ge(proj_out, GRP_AG + 1)
            for hp in range(2):
                g = GRP_GATE + hp
                group(g, ps[:, g % 4], [(wgate[:, hp * P:(hp + 1) * P], agT)])

            for i, (name, _) in enumerate(CH):
                if name == "v":
                    pe.wait_ge(kt_ready, 2)
                    for hp in range(2):
                        g = GRP["ktok"] + hp
                        pe.wait_ge(proj_out, g - 3)
                        for t in range(NT):
                            last = pe.transpose(ps[:, g % 4, t * P:(t + 1) * P], ktail[:, hp, t * P:(t + 1) * P], ident[:])
                        last.then_inc(proj, 1)
                    pe.wait_ge(proj_out, GRP["ktok"] + 2)
                    pe.wait_ge(turned_out, 3)
                    for c in range(7):
                        t, r = c // 2, GC * (c % 2)
                        bank, at = 4 + c % 2 + 2 * (t // 2), 256 * (t % 2)
                        for h in range(GH):
                            lo = 64 * (h % 2)
                            last = pe.matmul(ps[lo:lo + 64, bank, at + (h // 2) * P:at + (h // 2 + 1) * P],
                                             ktok[r:r + GC, t, h * 64:(h + 1) * 64], vg[r:r + GC, t, h * P:(h + 1) * P],
                                             start=True, stop=True)
                        last.then_inc(kv_done, 1)
                pe.wait_ge(wst_in[i % 2], 16 * (i // 2 + 1))
                for j in range(4):
                    g = GRP[name] + j
                    if name in ("qk_g", "q", "k"):
                        pairs = [(wst[:, i % 2, c, j * P:(j + 1) * P], aT[:, c]) for c in range(NC)]
                    else:
                        pairs = [(aT[:, c, j * P:(j + 1) * P], wst[:, i % 2, c]) for c in range(NC)]
                    group(g, ps[:, g % 4], pairs, proj)

            def mix_out(t, n, c):
                if c == 0:
                    pe.wait_ge(wst_in[n], 64)
                    pe.wait_ge(tm_out, t + 1)
                    pe.wait_ge(tg_out, t + 1)
                    if t >= 1 and n == 0:
                        pe.wait_ge(lg_out, t)
                    if 2 * t + n >= 1:
                        pe.wait_ge(h_ready, 2 * t + n)
                last = pe.matmul(ps[:, 3], actT[:, c, t * P:(t + 1) * P], wst[:, n, c], start=(c == 0), stop=(c == NC - 1))
                if c == NC - 1:
                    last.then_inc(wo_done, 1)

            def ffn_in(t):
                pe.wait_ge(f_ready, t + 1)
                for i in range(2):
                    if i == 0:
                        pe.wait_ge(om_out, min(t + 2, NT))
                    else:
                        pe.wait_ge(on_ready, min(t + 2, NT))
                    for c in range(4):
                        last = pe.transpose(ps[:, i, c * P:(c + 1) * P], F[:, (4 * i + c) * P:(4 * i + c + 1) * P], ident[:])
                    last.then_inc(ft_done, 1)
                pe.wait_ge(ft_out, 2 * t + 2)
                for c in range(NC):
                    pe.matmul(ps[:, 3, 0:NE], actT[:, c, t * P:(t + 1) * P], wr[:, c], start=(c == 0), stop=False)
                pe.matmul(ps[:, 3, 0:NE], ones[0:1, :], brow[:], start=False, stop=True).then_inc(lg_done, 1)

            pe.wait_ge(proj_out, NGRP)
            pe.wait_ge(gla_kq, 6)
            pe.wait_ge(consts, 17)
            for t in range(NT):
                tt = slice(t * P, (t + 1) * P)
                if t >= 1:
                    pe.wait_ge(on_ready, t)
                for h in range(GH):
                    last = pe.matmul(ps[:, 1, h * P:(h + 1) * P], kd[:, h // 2, tt], qz[:, h, tt], start=True, stop=True)
                last.then_inc(a_done, 1)
                for i in range(MH + 2):
                    if i < MH:
                        u, lo = t * MH + i, 64 * (i % 2)
                        if u >= 2:
                            pe.wait_ge(s_masked, u - 1)
                        else:
                            pe.wait_ge(st_ready, 14)
                        pe.matmul(ps[:, 4 + i % 2, 0:(t + 1) * P], qT[lo:lo + 64, i // 2, tt], kT[lo:lo + 64, i // 2, 0:(t + 1) * P],
                                  start=True, stop=True).then_inc(s_done, 1)
                    if t >= 1 and i < MH:
                        for c in range(2):
                            mix_out(t - 1, i // 4, 2 * (i % 4) + c)
                    if 1 <= i <= MH:
                        u = t * MH + i - 1
                        pe.wait_ge(p_exp, u + 1)
                        if u >= 2:
                            pe.wait_ge(pt_out, u - 1)
                        for k in range(t + 1):
                            last = pe.transpose(ps[:, 6 + u % 2, k * P:(k + 1) * P], Pm[:, u % 4, k * P:(k + 1) * P], ident[:])
                        last.then_inc(pt_done, 1)
                    if i >= 2:
                        h = i - 2
                        u = t * MH + h
                        pe.wait_ge(pt_out, u + 1)
                        if t >= 1 and h == 0:
                            pe.wait_ge(om_out, t)
                        for k in range(t + 1):
                            last = pe.matmul(ps[:, 0, h * 64:(h + 1) * 64], PTs[:, u % 2, k * P:(k + 1) * P], v_[:, k, h * 64:(h + 1) * 64],
                                             start=(k == 0), stop=(k == t))
                        last.then_inc(pv_done, 1)
                pe.wait_ge(a_out, t + 1)
                for h in range(GH):
                    for e in range(2):
                        c = 2 * t + e
                        pe.matmul(ps[e * GC:(e + 1) * GC, 1, h * P:(h + 1) * P], qz[:, h, c * GC:(c + 1) * GC], st[:, c, h // 2],
                                  start=True, stop=False)
                    last = pe.matmul(ps[:, 1, h * P:(h + 1) * P], AT[:, h * P:(h + 1) * P], vg[:, t, h * P:(h + 1) * P],
                                     start=False, stop=True)
                last.then_inc(go_done, 1)
                if t >= 1:
                    ffn_in(t - 1)
                pe.wait_ge(om_out, t + 1)
                if t >= 1:
                    pe.wait_ge(tg_out, t)
                for c in range(4):
                    last = pe.transpose(ps[:, 2, c * P:(c + 1) * P], OMS[:, c * P:(c + 1) * P], ident[:])
                last.then_inc(tm_done, 1)
                pe.wait_ge(on_ready, t + 1)
                pe.wait_ge(tm_out, t + 1)
                for c in range(4):
                    last = pe.transpose(ps[:, 2, c * P:(c + 1) * P], ON[:, c * P:(c + 1) * P], ident[:])
                last.then_inc(tg_done, 1)
            for n in range(2):
                for c in range(NC):
                    mix_out(NT - 1, n, c)
            ffn_in(NT - 1)
            pe.wait_ge(ple_ld, 32)
            for c in range(2):
                for t in range(NT):
                    last = pe.transpose(ps[:, 4 + c, t * P:(t + 1) * P], prow[:, t, c * P:(c + 1) * P], ident[:])
                last.then_inc(pt2_done, 1)
            pe.wait_ge(mk_ready, 1)
            for t in range(NT):
                for s in range(t):
                    pe.matmul(ps[:, 7, t * NE:(t + 1) * NE], ones[:], Mk[:, s], start=(s == 0), stop=False)
                pe.matmul(ps[:, 7, t * NE:(t + 1) * NE], before[:], Mk[:, t], start=(t == 0), stop=True)
            for t in range(NT):
                last = pe.matmul(ps[:, 7, NT * NE:(NT + 1) * NE], ones[:], Mk[:, t], start=(t == 0), stop=(t == NT - 1))
            last.then_inc(rank_done, 1)
            pe.wait_ge(pt2_out, 2)
            pe.wait_ge(lg_out, NT)

            def ple_tile(t):
                a = 2 * (t % 2)
                if t >= 2:
                    pe.wait_ge(pp_out, t - 1)
                for n in range(2):
                    for c in range(2):
                        last = pe.matmul(ps[:, a + n], pT[:, c, t * P:(t + 1) * P], wpp[:, c, n * 512:(n + 1) * 512],
                                         start=(c == 0), stop=(c == 1))
                last.then_inc(pp_done, 1)
            for t in range(NT):
                ple_tile(t)
            pe.wait_ge(oh_ready, 1)
            for a in range(NT * TOPK):
                last = pe.matmul(ps[0:CAP, 4, 0:NTAB], ohJ[:, a, :], ohB[:, a, :], start=(a == 0), stop=(a == NT * TOPK - 1))
            last.then_inc(tok_done, 1)

            def turn_x(b):
                pe.wait_ge(xg_in, b * 16 + 16)
                for c in range(NC):
                    last = pe.transpose(ps[:, 6 + c // 4, (c % 4) * CAP:(c % 4 + 1) * CAP], XG[:, c * P:(c + 1) * P], ident[0:CAP, 0:CAP])
                last.then_inc(xt_done, 1)

            def turn_y(b):
                pe.wait_ge(yt_ready, b * 2 + 2)
                for m in range(NC):
                    last = pe.transpose(ps[0:CAP, 6 + m // 4, (m % 4) * P:(m % 4 + 1) * P], YT[:, m, :], ident[:])
                last.then_inc(yr_done, 1)

            def expert_block(b, first):
                pe.wait_ge(xt_ready, b * 2 + 2)
                for q in range(4):
                    pe.wait_ge(w_in_s[q], b * 16 + 16)
                    if not first and q % 2 == 0:
                        pe.wait_ge(hid_done, b * 2 + (q // 2 - 1))
                    for jj in range(2):
                        j = 2 * q + jj
                        for s in range(2):
                            for c in range(NC):
                                last = pe.matmul(ps[:, 2 * (j // 4) + s, (j % 4) * CAP:(j % 4 + 1) * CAP],
                                                 w1q[:, q, c, 256 * jj + s:256 * (jj + 1):2], XT[:, c], start=(c == 0), stop=(c == NC - 1))
                    last.then_inc(w_used, 1)
                    if q == 1 and not first:
                        turn_y(b - 1)
                if not first:
                    pe.wait_ge(yr_out, b * 2)
                turn_x(b + 1)
                for f in range(NC):
                    if f % 4 == 0:
                        pe.wait_ge(w_in_s[4 + f // 4], b * 16 + 16)
                        pe.wait_ge(hid_done, b * 2 + (f // 4 + 1))
                    for m in range(NC):
                        last = pe.matmul(ps[:, 4 + m // 4, (m % 4) * CAP:(m % 4 + 1) * CAP], w2h[:, f, m * P:(m + 1) * P], HID[:, f],
                                         start=(f == 0 and m % 4 == 0), stop=(f == NC - 1), skip_group_check=True)
                    if f % 4 == 3:
                        last.then_inc(w_used, 1)

            pe.wait_ge(pp_out, NT)
            turn_x(0)
            expert_block(0, True)
            with pe.Fori(1, NE) as b:
                expert_block(b, False)
            n = extra_blocks(pe, lambda i: expert_block(i + NE, False))
            turn_y(n + (NE - 1))

            pe.wait_ge(wst_in[0], 80)
            pe.wait_ge(wst_in[1], 80)
            for t in range(NT):
                pe.wait_ge(h2_ready, t + 1)
                for i in range(2):
                    if t >= 1:
                        pe.wait_ge(h2t_out, 2 * t - 1 + i)
                    for c in range(4):
                        last = pe.transpose(ps[:, i, c * P:(c + 1) * P], H[:, t, (4 * i + c) * P:(4 * i + c + 1) * P], ident[:])
                    last.then_inc(h2t_done, 1)
                pe.wait_ge(h2t_out, 2 * t + 2)
                if t >= 2:
                    pe.wait_ge(gm_sig, t - 1)
                for n in range(2):
                    for c in range(NC):
                        last = pe.matmul(ps[:, 2 + 2 * (t % 2) + n], actT[:, c, t * P:(t + 1) * P], wst[:, n, c],
                                         start=(c == 0), stop=(c == NC - 1))
                last.then_inc(gm_done, 1)

        @block.vector
        def _(dve):
            made = [0]

            def link(ins):
                made[0] += 1
                ins.then_inc(dve_step, 1)
                dve.wait_ge(dve_step, made[0])

            def mean(i, src):
                return dve.tensor_scalar(ss[:, i:i + 1], src, 1.0 / D, EPS, ALU.mult, ALU.add)

            dve.wait_ge(turned, 1)
            dve.tensor_copy(vc[:], ps[:, 7, 0:19]).then_inc(turned_out, 1)
            dve.wait_ge(ms_ready, NT)
            dve.tensor_scalar(ss[:, 0:NT], ss[:, 0:NT], 1.0 / D, EPS, ALU.mult, ALU.add).then_inc(x_rstd, 1)
            dve.wait_ge(rstd_ready, 1)
            for t in range(NT):
                dve.tensor_scalar(xs[:, t], H[:, t], rstd[:, t:t + 1], None, ALU.mult).then_inc(xs_ready, 1)
            dve.wait_ge(turned, 2)
            dve.tensor_copy(b1T[:].rearrange("p c s e -> p (c s e)"), ps[:, 5]).then_inc(turned_out, 1)
            dve.tensor_copy(b2T[:].rearrange("p c e -> p (c e)"), ps[:, 6, 0:256]).then_inc(turned_out, 1)
            dve.wait_ge(gx_ready, 1)
            link(dve.tensor_scalar(G, G, 0.0, None, ALU.min))
            dve.wait_ge(gln, 1)
            link(dve.tensor_tensor(G, G, tmpG, ALU.subtract))
            dve.wait_ge(consts, 4)
            for hp in range(2):
                dve.tensor_tensor_scan(G[:, hp], keep, G[:, hp], 0.0, ALU.mult, ALU.add).then_inc(g_ready, 1)
            dve.wait_ge(g_ready, 2)
            for hp in range(2):
                gv = G[:, hp].rearrange("p (c s) -> p c s", s=GC)
                dve.tensor_tensor(ktail[:, hp].rearrange("p (c s) -> p c s", s=GC), gv[:, :, GC - 1:GC].to_broadcast([P, 8, GC]), gv,
                                  ALU.subtract).then_inc(dg_ready, 1)
            dve.wait_ge(proj_out, GRP["qk_g"] + 4)
            dve.wait_ge(eg_ready, 1)
            for h in range(GH):
                lo = 64 * (h % 2)
                dve.tensor_tensor(qz[lo:lo + 64, h], qraw[lo:lo + 64, h // 2], eG[lo:lo + 64, h // 2], ALU.mult).then_inc(gla_kq, 1)
            dve.wait_ge(eg_neg, 1)
            for hp in range(2):
                dve.tensor_tensor(kd[:, hp], kraw[:, hp], tmpG[:, hp], ALU.mult).then_inc(gla_kq, 1)
            dve.wait_ge(dg_exp, 1)
            for hp in range(2):
                dve.tensor_tensor(ktail[:, hp], ktail[:, hp], kraw[:, hp], ALU.mult).then_inc(kt_ready, 1)
            dve.wait_ge(consts, 16)
            dve.wait_ge(kv_done, 7)
            for c in range(7):
                bank, at = 4 + c % 2 + 2 * (c // 4), 256 * ((c // 2) % 2)
                if c >= 1:
                    dve.wait_ge(st_ready, 2 * c)
                for hp in range(2):
                    dve.scalar_tensor_tensor(out=st[:, c + 1, hp], in0=st[:, c, hp], scalar=eG[:, hp, c * GC + GC - 1:c * GC + GC],
                                             in1=ps[:, bank, at + hp * P:at + (hp + 1) * P], op0=ALU.mult, op1=ALU.add).then_inc(st_ready, 1)
            for t in range(NT):
                dve.wait_ge(proj_out, GRP["r"] + t + 1)
                dve.wait_ge(sig_r, t + 1)
                dve.tensor_tensor(rg[:, t], rg[:, t], tmpG[:, 0], ALU.mult).then_inc(rg_ready, 1)

            def add_mix(t, n):
                dve.wait_ge(wo_done, 2 * t + n + 1)
                dve.tensor_tensor(H[:, t, n * 512:(n + 1) * 512], H[:, t, n * 512:(n + 1) * 512], ps[:, 3], ALU.add).then_inc(h_ready, 1)

            def ffn_rows(t):
                dve.wait_ge(h_ss, t + 1)
                mean(4, ss[:, 4:5]).then_inc(h_ms, 1)
                dve.wait_ge(h_rs, t + 1)
                dve.tensor_scalar(F, H[:, t], rstd[:, 4:5], None, ALU.mult).then_inc(f_ready, 1)

            def ffn_turned(t):
                for i in range(2):
                    dve.wait_ge(ft_done, 2 * t + i + 1)
                    dve.tensor_tensor(actT[:, 4 * i:4 * i + 4, t * P:(t + 1) * P], ps[:, i].rearrange("p (c q) -> p c q", c=4),
                                      vc[:, 8 + 4 * i:12 + 4 * i].unsqueeze(2).to_broadcast([P, 4, P]), ALU.mult).then_inc(ft_out, 1)
                dve.wait_ge(lg_done, t + 1)
                dve.tensor_copy(L[:, t], ps[:, 3, 0:NE]).then_inc(lg_out, 1)
                dve.wait_ge(lg_out, t + 1)
                link(dve.max(top8[:, t], L[:, t]))
                link(dve.max_index(idx8[:, t], top8[:, t], L[:, t]))

            dve.wait_ge(consts, 17)
            for t in range(NT):
                n = (t + 1) * P
                dve.wait_ge(a_done, t + 1)
                if t >= 1:
                    dve.wait_ge(go_done, t)
                dve.copy_predicated(AT, chunk_ok[:].rearrange("p h q -> p (h q)"), ps[:, 1]).then_inc(a_out, 1)
                for h in range(MH):
                    u = t * MH + h
                    dve.wait_ge(s_done, u + 1)
                    if u >= 4:
                        dve.wait_ge(pt_done, u - 3)
                    dve.scalar_tensor_tensor(out=Pm[:, u % 4, 0:n], in0=dist[:, dbase[t]:dbase[t] + n], scalar=slope[h],
                                             in1=ps[:, 4 + h % 2, 0:n], op0=ALU.mult, op1=ALU.add).then_inc(s_masked, 1)
                    dve.wait_ge(s_masked, u + 1)
                    dve.tensor_reduce(nmax[:, u:u + 1], Pm[:, u % 4, 0:n], AX.X, ALU.max, negate=True).then_inc(m_ready, 1)
                    if t >= 1 and h == 3:
                        add_mix(t - 1, 0)
                if t >= 1:
                    add_mix(t - 1, 1)
                    ffn_rows(t - 1)
                dve.wait_ge(p_exp, (t + 1) * MH)
                link(dve.reciprocal(rinv[:, t * MH:(t + 1) * MH], rsum[:, t * MH:(t + 1) * MH]))
                dve.wait_ge(pv_done, (t + 1) * MH)
                if t >= 1:
                    dve.wait_ge(tm_done, t)
                dve.tensor_tensor(OMS.rearrange("p (h v) -> p h v", h=MH), ps[:, 0].rearrange("p (h v) -> p h v", h=MH),
                                  rinv[:, t * MH:(t + 1) * MH].unsqueeze(2).to_broadcast([P, MH, HD]), ALU.mult).then_inc(om_out, 1)
                dve.wait_ge(go_sq, t + 1)
                link(dve.tensor_reduce(ssg[:], ON.rearrange("p (h v) -> p h v", h=GH), AX.X, ALU.add))
                dve.tensor_scalar(ssg[:], ssg[:], 1.0 / P, EPS, ALU.mult, ALU.add).then_inc(go_ss, 1)
                dve.wait_ge(go_rs, t + 1)
                link(dve.tensor_tensor(ON.rearrange("p (h v) -> p h v", h=GH), ps[:, 1].rearrange("p (h v) -> p h v", h=GH),
                                       rsg[:].unsqueeze(2).to_broadcast([P, GH, P]), ALU.mult))
                dve.wait_ge(rg_ready, NT)
                dve.tensor_tensor(ON, ON, rg[:, t], ALU.mult).then_inc(on_ready, 1)
                if t >= 1:
                    ffn_turned(t - 1)
            add_mix(NT - 1, 0)
            add_mix(NT - 1, 1)
            ffn_rows(NT - 1)
            ffn_turned(NT - 1)

            A = NT * TOPK
            link(dve.tensor_copy(idxf[:], idx8[:, :, 0:TOPK]))
            link(dve.tensor_tensor(oh, it_b[:, 0:NE].unsqueeze(1).to_broadcast([P, A, NE]),
                                   idxf[:].rearrange("p t k -> p (t k)").unsqueeze(2).to_broadcast([P, A, NE]), ALU.is_equal))
            dve.tensor_reduce(Mk[:], oh.rearrange("p (t k) e -> p t e k", k=TOPK), AX.X, ALU.add).then_inc(mk_ready, 1)
            dve.tensor_tensor(ex4[:], top8[:, :, 0:TOPK], top8[:, :, 0:1].to_broadcast([P, NT, TOPK]), ALU.subtract).then_inc(e_in, 1)
            dve.wait_ge(e_out, 1)
            link(dve.tensor_reduce(s4[:], ex4[:], AX.X, ALU.add))
            link(dve.reciprocal(s4[:], s4[:]))
            link(dve.tensor_tensor(gate[:], ex4[:], s4[:].unsqueeze(2).to_broadcast([P, NT, TOPK]), ALU.mult))
            dve.wait_ge(rank_done, 1)
            link(dve.tensor_copy(cnt[:], ps[:, 7, NT * NE:(NT + 1) * NE]))
            link(dve.tensor_scalar(extra[:], cnt[:], CAP + 0.5, None, ALU.is_gt))
            for j in range(2, MAXFULL + 1):
                link(dve.scalar_tensor_tensor(out=extra[:], in0=cnt[:], scalar=j * CAP + 0.5, in1=extra[:], op0=ALU.is_gt, op1=ALU.add))
            link(dve.tensor_tensor_scan(xend[:], ones[:, 0:NE], extra[:], 0.0, ALU.mult, ALU.add))
            link(dve.tensor_tensor(xbase[:], xend[:], extra[:], ALU.subtract))
            link(dve.tensor_tensor(xbase[:], xbase[:], it_b[:, 0:NE], ALU.subtract))
            rank = ps[:, 7, 0:NT * NE].rearrange("p (t e) -> p t e", t=NT)
            link(dve.tensor_copy(Jm, rank))
            link(dve.tensor_scalar(full, Jm, CAP - 0.5, None, ALU.is_gt))
            link(dve.tensor_copy(has, full))
            for j in range(2, MAXFULL + 1):
                link(dve.scalar_tensor_tensor(out=full, in0=Jm, scalar=j * CAP - 0.5, in1=full, op0=ALU.is_gt, op1=ALU.add))
            link(dve.scalar_tensor_tensor(out=Jm, in0=full, scalar=-float(CAP), in1=Jm, op0=ALU.mult, op1=ALU.add))
            link(dve.tensor_scalar(xbase[:], xbase[:], float(NE - 1), None, ALU.add))
            link(dve.tensor_tensor(has, has, xbase[:].unsqueeze(1).to_broadcast([P, NT, NE]), ALU.mult))
            link(dve.tensor_tensor(has, has, full, ALU.add))
            link(dve.tensor_tensor(has, has, it_b[:, 0:NE].unsqueeze(1).to_broadcast([P, NT, NE]), ALU.add))
            for src, dst in ((has, Bs), (Jm, Js)):
                for t in range(NT):
                    pr = dve.tensor_tensor(prod[:, t * TOPK:(t + 1) * TOPK], oh[:, t * TOPK:(t + 1) * TOPK],
                                           src[:, t:t + 1].to_broadcast([P, TOPK, NE]), ALU.mult)
                link(pr)
                link(dve.tensor_reduce(dst[:], prod, AX.X, ALU.add))
            link(dve.tensor_tensor(ohB, it_b[:].unsqueeze(1).to_broadcast([P, A, NTAB]), Bs[:].unsqueeze(2).to_broadcast([P, A, NTAB]), ALU.is_equal))
            for t in range(NT):
                tt = ohB[:, t * TOPK:(t + 1) * TOPK]
                link(dve.tensor_scalar(tt, tt, tok[:, t:t + 1], None, ALU.mult))
            dve.tensor_tensor(ohJ, it_j[:].unsqueeze(1).to_broadcast([P, A, CAP]), Js[:].unsqueeze(2).to_broadcast([P, A, CAP]),
                              ALU.is_equal).then_inc(oh_ready, 1)
            link(dve.scalar_tensor_tensor(out=slotf[:], in0=Bs[:], scalar=float(CAP), in1=Js[:], op0=ALU.mult, op1=ALU.add))
            link(dve.tensor_copy(sloti[:], slotf[:]))
            link(dve.tensor_tensor(xcmp, it_b[0:1, 0:NEXTRA].unsqueeze(2).to_broadcast([1, NEXTRA, NE]),
                                   xend[0:1, :].unsqueeze(1).to_broadcast([1, NEXTRA, NE]), ALU.is_ge))
            link(dve.tensor_reduce(tabf[:, 0:NEXTRA], xcmp, AX.X, ALU.add))
            link(dve.tensor_scalar(tabf[:, 0:NEXTRA], tabf[:, 0:NEXTRA], float(NE - 1), None, ALU.min))
            link(dve.tensor_copy(tabf[:, NEXTRA:NEXTRA + 1], xend[0:1, NE - 1:NE]))
            link(dve.tensor_copy(tab[:], tabf[:]))
            dve.wait_ge(tok_done, 1)
            dve.tensor_copy(tokix[:], ps[0:CAP, 4, 0:NTAB]).then_inc(tab_ready, 1)

            def turned_x(b):
                dve.wait_ge(xt_done, b + 1)
                for i in range(2):
                    dve.tensor_tensor(XT[:, 4 * i:4 * i + 4], ps[:, 6 + i, 0:4 * CAP].rearrange("p (c j) -> p c j", c=4),
                                      vc[:, 8 + 4 * i:12 + 4 * i].unsqueeze(2).to_broadcast([P, 4, CAP]), ALU.mult).then_inc(xt_ready, 1)

            def expert_block(b, e, first=False):
                for hf in range(2):
                    s0 = 4 * hf
                    dve.wait_ge(w_used, b * WU + (2 * hf + 2))
                    bias = [b1T[:, 4 * hf:4 * hf + 4, s, bass.ds(e, 1)].to_broadcast([P, 4, CAP]) for s in range(2)]
                    hid = [ps[:, 2 * hf + s, 0:4 * CAP].rearrange("p (f j) -> p f j", f=4) for s in range(2)]
                    if hf == 1 or not first:
                        dve.wait_ge(hid_done, b * 2 + hf)
                    dve.tensor_tensor(T1, hid[0], bias[0], ALU.add).then_inc(moe_step, 1)
                    dve.tensor_tensor(T2, hid[1], bias[1], ALU.add).then_inc(moe_step, 1)
                    dve.wait_ge(moe_step, b * SWI + (s0 + 1))
                    dve.tensor_scalar(T1, T1, LIMIT, None, ALU.min).then_inc(glu_min, 1)
                    dve.wait_ge(moe_step, b * SWI + (s0 + 2))
                    dve.tensor_scalar(T2, T2, LIMIT, -LIMIT, ALU.min, ALU.max).then_inc(moe_step, 1)
                    dve.wait_ge(moe_step, b * SWI + (s0 + 3))
                    dve.wait_ge(glu_min, b * 2 + (hf + 1))
                    dve.scalar_tensor_tensor(out=T2, in0=T2, scalar=1.0, in1=T1, op0=ALU.add, op1=ALU.mult).then_inc(moe_step, 1)
                    dve.wait_ge(moe_step, b * SWI + (s0 + 4))
                    dve.wait_ge(sig_done, b * 2 + (hf + 1))
                    dve.tensor_tensor(HID[:, 4 * hf:4 * hf + 4], T2, SIG, ALU.mult).then_inc(hid_done, 1)
                turned_x(b + 1)
                dve.wait_ge(w_used, b * WU + WU)
                for i in range(2):
                    dve.tensor_tensor(YT[:, 4 * i:4 * i + 4], ps[:, 4 + i, 0:4 * CAP].rearrange("p (m j) -> p m j", m=4),
                                      b2T[:, 4 * i:4 * i + 4, bass.ds(e, 1)].to_broadcast([P, 4, CAP]), ALU.add).then_inc(yt_ready, 1)

            turned_x(0)
            expert_block(0, 0, True)
            with dve.Fori(1, NE) as b:
                expert_block(b, b)

            def body(i):
                e = dve.value_load(tab[0:1, bass.ds(i, 1)], min_val=0, max_val=NE - 1)
                expert_block(i + NE, e)
            extra_blocks(dve, body)

            def tail(t):
                dve.wait_ge(gm_sig, t + 1)
                if t == 0:
                    dve.wait_ge(tail_in, 32)
                link(dve.tensor_tensor(SG[:, t % 2], SG[:, t % 2], ple_in[:, t], ALU.mult))
                dve.tensor_tensor(H[:, t], H[:, t], SG[:, t % 2], ALU.add).then_inc(h3_ready, 1)

            def last_norm(t):
                dve.wait_ge(h3_ss, t + 1)
                mean(6, ssg[:, t:t + 1]).then_inc(h3_ms, 1)
                dve.wait_ge(h3_rs, t + 1)
                dve.scalar_tensor_tensor(out=OUTB[:, t % 2], in0=H[:, t], scalar=rstd[:, 6:7], in1=gfin, op0=ALU.mult,
                                         op1=ALU.mult).then_inc(o_ready, 1)

            for t in range(NT + 1):
                if t < NT:
                    dve.wait_ge(yg_in[t], 16 * TOPK)
                    for k in range(TOPK):
                        ins = dve.scalar_tensor_tensor(out=H[:, t], in0=yg[:, t * TOPK + k], scalar=gate[:, t, k:k + 1], in1=H[:, t],
                                                       op0=ALU.mult, op1=ALU.add)
                        if k < TOPK - 1:
                            link(ins)
                        else:
                            ins.then_inc(h2_ready, 1)
                if t >= 1:
                    tail(t - 1)
                    last_norm(t - 1)



_INS = ['x', 'p', 'g_mix', 'w_in', 'w_gla_gate', 'b_gla_gate', 'g_gla_norm', 'w_out', 'g_ffn', 'w_router', 'b_router',
        'w1', 'b1', 'w2', 'b2', 'w_ple_gate', 'w_ple_proj', 'g_ple', 'g_final']
_OUTS = [((1, 512, 1024), 'float32')]


def kernel(**inputs):
    import numpy as _np
    import concourse.bacc as _bacc
    from concourse import mybir as _mybir
    from concourse.bass_utils import run_bass_kernel_spmd as _run

    nc = _bacc.Bacc("TRN2", target_bir_lowering=False, num_devices=1)
    arrays, args = {}, []
    for name in _INS:
        a = _np.ascontiguousarray(inputs[name])
        arrays[f"in_{name}_dram"] = a
        args.append(nc.dram_tensor(f"in_{name}_dram", a.shape, _mybir.dt.from_np(a.dtype), kind="ExternalInput").ap())
    for i, (shape, dtype) in enumerate(_OUTS):
        dt = _mybir.dt.from_np(_np.dtype(dtype))
        args.append(nc.dram_tensor(f"out_{i}_dram", shape, dt, kind="ExternalOutput").ap())
    hybrid_layer(nc, *args)
    r = _run(nc, [arrays], core_ids=[0])
    return r.results[0]["out_0_dram"]
```

```python
from contextlib import ExitStack

import concourse.bass as bass
from concourse import mybir

F32 = mybir.dt.float32
I32 = mybir.dt.int32
U32 = mybir.dt.uint32
U8 = mybir.dt.uint8
F32R = mybir.dt.float32r
ALU = mybir.AluOpType
ACT = mybir.ActivationFunctionType
AX = mybir.AxisListType

P = 128
SEQ = 512
D = 1024
NT = SEQ // P
NC = D // P
HD = 64
MH = 8
GH = 4
GC = 64
RANK = 16
TAU = 16.0
NE = 32
TOPK = 4
CAP = 96
NEXTRA = SEQ * TOPK // CAP
NBLK = NE + NEXTRA
NTAB = NBLK + 1
MAXFULL = (SEQ - 1) // CAP
LIMIT = 7.0
ALPHA = 1.702
EPS = 1e-6
MASKED = -1.0e30
WU = 6
PIECES = 16
RING = 4
SWI = 8
PLE = 256


def hybrid_layer(nc, x, p, g_mix, w_in, w_gla_gate, b_gla_gate, g_gla_norm, w_out, g_ffn, w_router, b_router,
                 w1, b1, w2, b2, w_ple_gate, w_ple_proj, g_ple, g_final, out):
    ctx = ExitStack()
    with ctx:
        def sb(name, shape, dt=F32):
            return ctx.enter_context(nc.sbuf_tensor(name, shape, dt))

        def sem(name):
            return ctx.enter_context(nc.semaphore(name))

        f_rows = nc.dram_tensor("f_rows", (SEQ, D), F32, kind="Internal").ap()
        y_rows = nc.dram_tensor("y_rows", (NBLK * CAP, D), F32, kind="Internal").ap()
        ple_rows = nc.dram_tensor("ple_rows", (SEQ, D), F32, kind="Internal").ap()

        def scope(*shapes):
            with ExitStack() as held_here:
                return [held_here.enter_context(nc.sbuf_tensor(name, shape, dt)) for name, shape, dt in shapes]

        aTl, _, PWh, aTh = scope(("aTl", [P, NC, SEQ], F32R), ("skip0", [P, 24576 - NC * SEQ], F32),
                                 ("PWh", [P, NC, 512], F32R), ("aTh", [P, NC, SEQ], F32R))

        W = sb("W", [P, 24576])
        w1q = W[:, 0:16384].rearrange("p (q c n) -> p q c n", q=4, c=NC)
        w2h = W[:, 16384:24576].rearrange("p (f n) -> p f n", f=NC)

        def in_w(at, *shape):
            n = 1
            for s in shape:
                n *= s
            v = W[:, at:at + n]
            return v.rearrange("p (a b) -> p a b", a=shape[0]) if len(shape) == 2 else v

        qT = in_w(4096, 4, SEQ)
        kT = in_w(6144, 4, SEQ)
        xs = in_w(4096, NT, D)
        v_ = in_w(8192, NT, 512)
        vg = in_w(10240, NT, 512)
        rg = in_w(12288, NT, 512)
        qz = in_w(14336 + 1024, GH, SEQ)
        kd = in_w(17408, 2, SEQ)
        qraw = in_w(18432, 2, SEQ)
        kraw = in_w(19456, 2, SEQ)
        G = in_w(20480, 2, SEQ)
        eG = in_w(21504, 2, SEQ)
        tmpG = in_w(22528, 2, SEQ)
        ktok = in_w(23552, NT, 256)
        ktail = in_w(14336, 2, SEQ)
        yg = in_w(0, 16, D)
        ple_in = in_w(16384, NT, D)
        gfin = W[:, 20480:21504]
        gple = W[:, 21504:22528]

        H = sb("H", [P, NT, D])
        actT = sb("actT", [P, NC, SEQ])
        b12raw = actT[:].rearrange("p c n -> p (c n)")[0:2 * NE, 0:3 * D]

        ident = sb("ident", [P, P])
        before = sb("before", [P, P])
        ones = sb("ones", [P, P])
        it_j = sb("it_j", [P, CAP])
        it_b = sb("it_b", [P, NTAB])
        tok = sb("tok", [P, NT])
        mhalf = sb("mhalf", [P, 8])
        vc = sb("vc", [P, 19])
        brow = sb("brow", [1, NE])
        pair = sb("pair", [2 * NE, NE])
        ss = sb("ss", [P, 8])
        rstd = sb("rstd", [P, 8])
        ssg = sb("ssg", [P, GH])
        rsg = sb("rsg", [P, GH])
        nmax = sb("nmax", [P, NT * MH])
        rsum = sb("rsum", [P, NT * MH])
        rinv = sb("rinv", [P, NT * MH])
        L = sb("L", [P, NT, NE])
        top8 = sb("top8", [P, NT, 8])
        idx8 = sb("idx8", [P, NT, 8], U32)
        idxf = sb("idxf", [P, NT, TOPK])
        ex4 = sb("ex4", [P, NT, TOPK])
        gate = sb("gate", [P, NT, TOPK])
        s4 = sb("s4", [P, NT])
        Mk = sb("Mk", [P, NT, NE])
        PX = sb("PX", [P, NT + 1, NE])
        cnt = sb("cnt", [P, NE])
        extra = sb("extra", [P, NE])
        xend = sb("xend", [P, NE])
        xbase = sb("xbase", [P, NE])
        Bs = sb("Bs", [P, NT * TOPK])
        Js = sb("Js", [P, NT * TOPK])
        slotf = sb("slotf", [P, NT * TOPK])
        sloti = sb("sloti", [P, NT * TOPK], I32)
        tokix = sb("tokix", [CAP, NTAB], I32)
        held = sb("held", [1, 1])
        tabf = sb("tabf", [1, NEXTRA + 1])
        tab = sb("tab", [1, NEXTRA + 1], I32)

        dist, chunk_ok, wag, wgate, wr, AT, OMS, M, wst = scope(
            ("dist", [P, 1280], F32),
            ("chunk_ok", [P, GH, P], U8),
            ("wag", [P, NC, RANK], F32), ("wgate", [RANK, 256], F32), ("wr", [P, NC, NE], F32),
            ("AT", [P, 512], F32), ("OMS", [P, 512], F32), ("M", [P, 6656], F32),
            ("wst", [P, 2, NC, 512], F32))
        AT, OMS = AT[:], OMS[:]
        _, wagh, wagl, _, PWl = scope(("skip1", [P, 3712], F32), ("wagh", [P, NC, RANK], F32R), ("wagl", [P, NC, RANK], F32R),
                                      ("skip2", [P, 9856], F32), ("PWl", [P, NC, 512], F32R))
        wpp = wst[:, 0, 0:4, :].rearrange("p a b -> p (a b)").rearrange("p (c n) -> p c n", c=2)
        prow = wst[:, 0, 4:6, :].rearrange("p a b -> p (a b)").rearrange("p (t n) -> p t n", t=NT)
        pT = wst[:, 0, 6:8, :]
        pleo = wst[:, 1, :, :].rearrange("p a b -> p (a b)").rearrange("p (t n) -> p t n", t=NT)
        Pm = M[:, 0:2048].rearrange("p (b n) -> p b n", b=4)
        PTs = M[:, 2048:3072].rearrange("p (b n) -> p b n", b=2)
        vraw = M[0:19, 0:P]
        keep = M[:, 128:640]
        agT = M[0:RANK, 2048:2560]
        ON = M[:, 3072:3584]
        st = M[:, 3584:5632].rearrange("p (c h n) -> p c h n", c=8, h=2)
        F = M[:, 5632:6656]
        zero = M[0:CAP, 5632:6656]
        oh = M[:, 0:512].rearrange("p (a e) -> p a e", e=NE)
        prod = M[:, 512:1024].rearrange("p (a e) -> p a e", e=NE)
        ohJ = M[:, 1024:2560].rearrange("p (a j) -> p a j", j=CAP)
        ohB = M[:, 2560:2560 + 16 * NTAB].rearrange("p (a b) -> p a b", b=NTAB)
        xcmp = M[0:1, 3584:3584 + NEXTRA * NE].rearrange("p (b e) -> p b e", b=NEXTRA)
        full, has, Jm = (M[:, a:a + NT * NE].rearrange("p (t e) -> p t e", t=NT) for a in (4256, 4384, 4512))

        BB, M2, XTh, XTl, sel, WS = scope(
            ("BB", [2 * NE, 3 * D], F32R),
            ("M2", [P, 5376], F32),
            ("XTh", [P, NC, CAP], F32R), ("XTl", [P, NC, CAP], F32R),
            ("sel", [2 * NE, CAP], F32R),
            ("WS", [P, RING, 2, 2, 512], F32R))
        HIDT = M2[:, 0:768].rearrange("p (f j) -> p f j", f=NC)
        T1, T2, SIG = M2[0:CAP, 768:1024], M2[0:CAP, 1024:1280], M2[0:CAP, 1280:1536]
        HIDr = M2[0:CAP, 1536:2560]
        YR = M2[0:CAP, 2560:3584]
        XTf = M2[:, 3584:4352].rearrange("p (c j) -> p c j", c=NC)
        XG = M2[0:CAP, 4352:5376]

        TL, wpg = scope(("TL", [P, 10080], F32), ("wpg", [P, 2, NC, 512], F32))
        SG = TL[:, 0:2048].rearrange("p (b n) -> p b n", b=2)
        OUTB = TL[:, 2048:4096].rearrange("p (b n) -> p b n", b=2)

        ps = ctx.enter_context(nc.psum_tensor("ps", [P, 8, 512], F32))

        x_in = [sem(f"x_in{t}") for t in range(NT)]
        vec_in = sem("vec_in")
        small_in = sem("small_in")
        bias_in = sem("bias_in")
        wst_in = [sem("wst_in0"), sem("wst_in1")]
        ple_ld = sem("ple_ld")
        w_in_s = [sem(f"w_unit_in{u}") for u in range(WU)]
        consts = sem("consts")
        pool_step = sem("pool_step")
        act_step = sem("act_step")
        dve_step = sem("dve_step")
        turned = sem("turned")
        turned_out = sem("turned_out")
        x_rstd = sem("x_rstd")
        ms_ready = sem("ms_ready")
        rstd_ready = sem("rstd_ready")
        xs_ready = sem("xs_ready")
        proj = sem("proj")
        at_lo = sem("at_lo")
        wag_hi = sem("wag_hi")
        wag_lo = sem("wag_lo")
        p_hi = sem("p_hi")
        p_lo = sem("p_lo")
        p_used = sem("p_used")
        x_back = sem("x_back")
        proj_out = sem("proj_out")
        gx_ready = sem("gx_ready")
        gabs = sem("gabs")
        gln = sem("gln")
        g_ready = sem("g_ready")
        eg_ready = sem("eg_ready")
        eg_neg = sem("eg_neg")
        dg_ready = sem("dg_ready")
        dg_exp = sem("dg_exp")
        kt_ready = sem("kt_ready")
        gla_kq = sem("gla_kq")
        kv_done = sem("kv_done")
        st_ready = sem("st_ready")
        sig_r = sem("sig_r")
        rg_ready = sem("rg_ready")
        a_done = sem("a_done")
        a_out = sem("a_out")
        s_done = sem("s_done")
        s_masked = sem("s_masked")
        m_ready = sem("m_ready")
        p_exp = sem("p_exp")
        pt_done = sem("pt_done")
        pt_out = sem("pt_out")
        pv_done = sem("pv_done")
        om_out = sem("om_out")
        go_done = sem("go_done")
        go_sq = sem("go_sq")
        go_ss = sem("go_ss")
        go_rs = sem("go_rs")
        on_ready = sem("on_ready")
        tm_done = sem("tm_done")
        tm_out = sem("tm_out")
        tg_done = sem("tg_done")
        tg_out = sem("tg_out")
        wo_done = sem("wo_done")
        h_ready = sem("h_ready")
        h_ss = sem("h_ss")
        h_ms = sem("h_ms")
        h_rs = sem("h_rs")
        f_ready = sem("f_ready")
        f_stored = sem("f_stored")
        ft_done = sem("ft_done")
        ft_out = sem("ft_out")
        lg_done = sem("lg_done")
        lg_out = sem("lg_out")
        e_in = sem("e_in")
        e_out = sem("e_out")
        mk_ready = sem("mk_ready")
        rank_done = sem("rank_done")
        oh_ready = sem("oh_ready")
        tok_done = sem("tok_done")
        tab_ready = sem("tab_ready")
        slot_ready = sem("slot_ready")
        pt2_done = sem("pt2_done")
        pt2_out = sem("pt2_out")
        pp_done = sem("pp_done")
        pp_ss = sem("pp_ss")
        pp_ms = sem("pp_ms")
        pp_rs = sem("pp_rs")
        pp_out = sem("pp_out")
        ple_scaled = sem("ple_scaled")
        ple_stored = sem("ple_stored")
        blocks_done = sem("blocks_done")
        xg_in = sem("xg_in")
        zero_ready = sem("zero_ready")
        y_zeroed = sem("y_zeroed")
        xt_done = sem("xt_done")
        xt_ready = sem("xt_ready")
        xh_ready = sem("xh_ready")
        xl_ready = sem("xl_ready")
        bb_hi = sem("bb_hi")
        bb_ready = sem("bb_ready")
        sel_ready = sem("sel_ready")
        pair_ready = sem("pair_ready")
        w_hi = sem("w_hi")
        w_lo = sem("w_lo")
        piece_used = sem("piece_used")
        w2_used = sem("w2_used")
        h1_done = sem("h1_done")
        moe_step = sem("moe_step")
        glu_min = sem("glu_min")
        sig_done = sem("sig_done")
        hid_ready = sem("hid_ready")
        th_done = sem("th_done")
        ht_out = sem("ht_out")
        y_done = sem("y_done")
        yr_out = sem("yr_out")
        y_stored = sem("y_stored")
        yg_in = [sem(f"yg_in{s}") for s in range(NT * TOPK)]
        tail_in = sem("tail_in")
        h2_ready = sem("h2_ready")
        h2t_done = sem("h2t_done")
        h2t_out = sem("h2t_out")
        gm_done = sem("gm_done")
        gm_sig = sem("gm_sig")
        h3_ready = sem("h3_ready")
        h3_ss = sem("h3_ss")
        h3_ms = sem("h3_ms")
        h3_rs = sem("h3_rs")
        o_ready = sem("o_ready")
        o_stored = [sem("o_stored0"), sem("o_stored1")]

        CH = [("qk_g", 1536), ("v_g", 2048), ("q", 0), ("k", 512), ("v", 1024), ("r", 2560)]
        w_in_v = w_in[0].rearrange("(c p) n -> p c n", p=P)

        GRP_AG = 8
        GRP_GATE = 9
        GRP = {"qk_g": 11, "v_g": 15, "q": 19, "k": 23, "ktok": 27, "v": 29, "r": 33}
        NGRP = 37
        slope = [2.0 ** (-8.0 * (h + 1) / MH) for h in range(MH)]
        dbase = [0, 128, 384, 768]

        def load_expert(sp, b, e, guard, units=range(WU)):
            for u in units:
                if u < 4:
                    if guard:
                        sp.wait_ge(w_lo, b * PIECES + (4 * (u + 1) - PIECES))
                    src = w1[0, bass.ds(e, 1), :, u * 512:(u + 1) * 512].rearrange("o (c p) n -> p (o c) n", p=P)
                    sp.dma_start(w1q[:, u], src).then_inc(w_in_s[u], 16)
                else:
                    k = u - 4
                    if guard:
                        sp.wait_ge(w2_used, b * 2 + (k - 1))
                    src = w2[0, bass.ds(e, 1), k * 512:(k + 1) * 512, :].rearrange("o (c p) n -> p (o c) n", p=P)
                    sp.dma_start(w2h[:, 4 * k:4 * k + 4], src).then_inc(w_in_s[u], 16)

        def extra_blocks(eng, body):
            n = eng.value_load(tab[0:1, NEXTRA:NEXTRA + 1], min_val=0, max_val=NEXTRA)
            with eng.If(n > 0):
                with eng.Fori(0, n) as i:
                    body(i)
            return n

        block = ctx.enter_context(nc.Block())

        @block.sync
        def _(sp):
            for t in range(NT):
                sp.dma_start(H[:, t], x[0, t * P:(t + 1) * P, :]).then_inc(x_in[t], 16)
            sp.dma_start(vraw[0:8, :], g_mix[0].rearrange("(c p) -> c p", p=P)).then_inc(vec_in, 16)
            sp.dma_start(vraw[8:16, :], g_ffn[0].rearrange("(c p) -> c p", p=P)).then_inc(vec_in, 16)
            sp.dma_start(vraw[16:18, :], b_gla_gate[0].rearrange("(c p) -> c p", p=P)).then_inc(vec_in, 16)
            sp.dma_start(vraw[18:19, :], g_gla_norm).then_inc(vec_in, 16)
            sp.dma_start(wag[:], w_in_v[:, :, 3072:3088]).then_inc(vec_in, 16)
            for i in range(6):
                if i >= 1:
                    sp.wait_ge(p_lo, 4 * i)
                sp.dma_start(wst[:, 0], w_in_v[:, :, CH[i][1]:CH[i][1] + 512]).then_inc(wst_in[0], 16)
            sp.wait_ge(zero_ready, 1)
            sp.dma_start(y_rows[NE * CAP:, :].rearrange("(i r) n -> r i n", r=CAP), zero.unsqueeze(1).to_broadcast([CAP, NEXTRA, D])).then_inc(y_zeroed, 16)
            wo_v = w_out[0].rearrange("(c p) n -> p c n", p=P)
            for n in range(2):
                if n == 0:
                    sp.wait_ge(p_lo, 24)
                else:
                    sp.wait_ge(proj, NGRP)
                    for t in range(NT):
                        sp.dma_start(H[:, t], x[0, t * P:(t + 1) * P, :]).then_inc(x_back, 16)
                sp.dma_start(wst[:, n], wo_v[:, :, n * 512:(n + 1) * 512]).then_inc(wst_in[n], 16)
            sp.wait_ge(tg_done, NT)
            sp.wait_ge(on_ready, NT)
            load_expert(sp, 0, 0, False, range(0, 2))
            sp.wait_ge(ple_ld, 32)
            load_expert(sp, 0, 0, False, range(2, 4))
            for t in range(NT):
                sp.wait_ge(pp_out, t + 1)
                sp.dma_start(ple_rows[t * P:(t + 1) * P, :], pleo[:, t]).then_inc(ple_stored, 16)
            load_expert(sp, 0, 0, False, range(4, WU))
            with sp.Fori(1, NE) as b:
                load_expert(sp, b, b, True)
            sp.wait_ge(tab_ready, 1)

            def body(i):
                e = sp.value_load(tab[0:1, bass.ds(i, 1)], min_val=0, max_val=NE - 1)
                load_expert(sp, i + NE, e, True)
            n = extra_blocks(sp, body)
            sp.wait_ge(piece_used, (n + NE) * PIECES)
            wg_v = w_ple_gate[0].rearrange("(c p) n -> p c n", p=P)
            for i in range(2):
                sp.dma_start(wpg[:, i], wg_v[:, :, i * 512:(i + 1) * 512]).then_inc(wst_in[i], 16)
            sp.wait_ge(yg_in[TOPK - 1], 16)
            sp.dma_start(ple_in, ple_rows.rearrange("(t p) n -> p t n", p=P)).then_inc(tail_in, 16)
            sp.dma_start(gple, g_ple[0].partition_broadcast(P)).then_inc(tail_in, 16)
            sp.dma_start(gfin, g_final.partition_broadcast(P)).then_inc(tail_in, 16)
            for t in range(NT):
                sp.wait_ge(o_ready, t + 1)
                sp.dma_start(out[0, t * P:(t + 1) * P, :], OUTB[:, t % 2]).then_inc(o_stored[t % 2], 16)
            for i in range(2):
                sp.wait_ge(o_stored[i], 16 * (NT // 2))

        @block.gpsimd
        def _(pool):
            made = [0]

            def link(ins):
                made[0] += 1
                ins.then_inc(pool_step, 1)
                pool.wait_ge(pool_step, made[0])

            consts_made = [0]

            def const(ins):
                consts_made[0] += 1
                ins.then_inc(consts, 1)
                pool.wait_ge(consts, consts_made[0])

            pool.dma_start(wgate[:], w_gla_gate[0]).then_inc(small_in, 16)
            pool.dma_start(wr[:], w_router[0].rearrange("(c p) n -> p c n", p=P)).then_inc(small_in, 16)
            pool.dma_start(brow[:], b_router).then_inc(small_in, 16)
            link(pool.memset(ident[:], 0.0))
            const(pool.affine_select(out=ident[:], in_=ident[:], compare_op=ALU.not_equal, fill=1.0, base=0,
                               pattern=[[-1, P]], channel_multiplier=1))
            const(pool.memset(mhalf[:], -0.5))
            pool.wait_ge(x_rstd, 1)
            pool.tensor_tensor(rstd[:, 0:NT], ss[:, 0:NT], mhalf[:, 0:NT], ALU.pow).then_inc(rstd_ready, 1)
            pool.wait_ge(rstd_ready, 1)
            link(pool.memset(ones[:], 1.0))
            const(pool.affine_select(out=before[:], in_=ones[:], compare_op=ALU.is_gt, fill=0.0, base=0,
                               pattern=[[1, P]], channel_multiplier=-1))
            link(pool.memset(keep, 1.0))
            const(pool.memset(keep[:, 0:SEQ:GC], 0.0))
            link(pool.iota(dist[:, 0:512], [[0, GH], [1, P]], base=1, channel_multiplier=-1, allow_small_or_imprecise_dtypes=True))
            link(pool.tensor_scalar(dist[:, 0:512], dist[:, 0:512], 0.0, None, ALU.max))
            link(pool.tensor_scalar(dist[:, 0:512], dist[:, 0:512], 1.0, None, ALU.min))
            for h in range(GH):
                link(pool.memset(dist[0:GC, h * P + GC:(h + 1) * P], 0.0))
            link(pool.tensor_copy(chunk_ok[:], dist[:, 0:512].rearrange("p (h q) -> p h q", h=GH)))
            for t in range(NT):
                n = (t + 1) * P
                dt_ = dist[:, dbase[t]:dbase[t] + n]
                link(pool.iota(dt_, [[1, n]], base=-t * P, channel_multiplier=-1, allow_small_or_imprecise_dtypes=True))
                const(pool.affine_select(out=dt_, in_=dt_, compare_op=ALU.is_ge, fill=MASKED * 256.0, base=t * P,
                                   pattern=[[-1, n]], channel_multiplier=1))
            const(pool.iota(it_j[:], [[1, CAP]], base=0, channel_multiplier=0, allow_small_or_imprecise_dtypes=True))
            const(pool.iota(it_b[:], [[1, NTAB]], base=0, channel_multiplier=0, allow_small_or_imprecise_dtypes=True))
            const(pool.iota(tok[:], [[P, NT]], base=0, channel_multiplier=1, allow_small_or_imprecise_dtypes=True))
            for h in range(GH):
                lo = 64 * (1 - h % 2)
                const(pool.memset(qz[lo:lo + 64, h, :], 0.0))
            const(pool.memset(st[:, 0], 0.0))
            const(pool.memset(AT, 0.0))
            pool.memset(zero, 0.0).then_inc(zero_ready, 1)

            def go_rstd(t):
                pool.wait_ge(go_ss, t + 1)
                pool.tensor_tensor(rsg[:], ssg[:], mhalf[:, 0:GH], ALU.pow).then_inc(go_rs, 1)

            def h_rstd(t):
                pool.wait_ge(h_ms, t + 1)
                pool.tensor_tensor(rstd[:, 4:5], ss[:, 4:5], mhalf[:, 0:1], ALU.pow).then_inc(h_rs, 1)

            for t in range(NT):
                go_rstd(t)
                if t > 0:
                    h_rstd(t - 1)
            h_rstd(NT - 1)
            for t in range(NT):
                pool.wait_ge(pp_ss, t + 1)
                link(pool.tensor_scalar(ss[:, 5:6], ss[:, 7:8], 1.0 / D, EPS, ALU.mult, ALU.add))
                pool.tensor_tensor(rstd[:, 5:6], ss[:, 5:6], mhalf[:, 0:1], ALU.pow).then_inc(pp_rs, 1)
                pool.wait_ge(pp_rs, t + 1)

            def gather(b):
                if b > 0:
                    pool.wait_ge(xt_done, b)
                pool.indirect_dma_start(XG, None, f_rows, bass.IndirectOffsetOnAxis(ap=tokix[:, b:b + 1].bitcast(U32), axis=0)).then_inc(xg_in, 16)

            pool.wait_ge(tab_ready, 1)
            for b in range(NE + 1):
                gather(b)
            n = pool.value_load(tab[0:1, NEXTRA:NEXTRA + 1], min_val=0, max_val=NEXTRA)
            for i in range(NEXTRA):
                with pool.If(n > i):
                    gather(NE + 1 + i)
            pool.wait_ge(blocks_done, 1)
            for t in range(NT):
                for k in range(TOPK):
                    s = t * TOPK + k
                    pool.indirect_dma_start(yg[:, s], None, y_rows, bass.IndirectOffsetOnAxis(ap=sloti[:, s:s + 1].bitcast(U32), axis=0)).then_inc(yg_in[s], 16)
            pool.wait_ge(tail_in, 48)
            for t in range(NT):
                pool.tensor_tensor(ple_in[:, t], ple_in[:, t], gple, ALU.mult).then_inc(ple_scaled, 1)
            pool.wait_ge(ple_scaled, NT)
            for t in range(NT):
                pool.wait_ge(h3_ms, t + 1)
                pool.tensor_tensor(rstd[:, 6:7], ss[:, 6:7], mhalf[:, 0:1], ALU.pow).then_inc(h3_rs, 1)

        @block.scalar
        def _(act):
            for t in range(NT):
                act.wait_ge(x_in[t], 16)
                act.activation(xs[:, t], H[:, t], ACT.Square, accum_out=ss[:, t:t + 1]).then_inc(ms_ready, 1)

            act.wait_ge(turned_out, 1)
            for g in range(NC):
                act.wait_ge(proj, g + 1)
                act.activation(aTh[:, g], ps[:, g % 4], ACT.Copy, scale=vc[:, g:g + 1]).then_inc(proj_out, 1)
                if g == 3:
                    act.wait_ge(vec_in, 80)
                    act.activation(wagh[:], wag[:], ACT.Copy).then_inc(wag_hi, 1)

            def upper(i):
                act.wait_ge(wst_in[0], 16 * (i + 1))
                for k in range(4):
                    if i == 0:
                        act.wait_ge(xs_ready, NT)
                    elif k < 3:
                        act.wait_ge(p_used, 3 * (i - 1) + k + 1)
                    else:
                        act.wait_ge(proj, GRP[CH[i - 1][0]] + 4)
                    act.activation(PWh[:, 2 * k:2 * k + 2], wst[:, 0, 2 * k:2 * k + 2], ACT.Copy).then_inc(p_hi, 1)

            def evac(g, dst, scale=1.0):
                act.wait_ge(proj, g + 1)
                act.activation(dst, ps[0:dst.shape[0], g % 4], ACT.Copy, scale=scale).then_inc(proj_out, 1)

            upper(0)
            evac(GRP_AG, agT)
            for hp in range(2):
                act.wait_ge(proj, GRP_GATE + hp + 1)
                act.activation(G[:, hp], ps[:, (GRP_GATE + hp) % 4], ACT.Identity, bias=vc[:, 16 + hp:17 + hp]).then_inc(proj_out, 1)
            act.wait_ge(proj_out, GRP_GATE + 2)
            act.activation(tmpG, G, ACT.Abs).then_inc(gx_ready, 1)
            act.wait_ge(gx_ready, 1)
            act.activation(tmpG, tmpG, ACT.Exp, scale=-1.0).then_inc(gabs, 1)
            act.wait_ge(gabs, 1)
            act.activation(tmpG, tmpG, ACT.Ln, bias=1.0).then_inc(gln, 1)
            for i in range(4):
                if i == 3:
                    upper(1)
                dst = qraw[:, i] if i < 2 else kraw[:, i - 2]
                evac(GRP["qk_g"] + i, dst, HD ** -0.5 if i < 2 else 1.0)
            act.wait_ge(g_ready, 2)
            act.activation(eG, G, ACT.Exp, scale=1.0 / TAU).then_inc(eg_ready, 1)
            act.activation(tmpG, G, ACT.Exp, scale=-1.0 / TAU).then_inc(eg_neg, 1)
            for t in range(NT):
                if t == 3:
                    upper(2)
                evac(GRP["v_g"] + t, vg[:, t])
            act.wait_ge(dg_ready, 2)
            act.activation(ktail, ktail, ACT.Exp, scale=1.0 / TAU).then_inc(dg_exp, 1)
            for i in range(4):
                if i == 3:
                    upper(3)
                evac(GRP["q"] + i, qT[:, i], HD ** -0.5)
            for i in range(4):
                if i == 3:
                    upper(4)
                evac(GRP["k"] + i, kT[:, i])
            for hp in range(2):
                act.wait_ge(proj, GRP["ktok"] + hp + 1)
                act.activation(ktok[:, :, hp * P:(hp + 1) * P], ps[:, (GRP["ktok"] + hp) % 4].rearrange("p (t f) -> p t f", t=NT),
                               ACT.Copy).then_inc(proj_out, 1)
            for t in range(NT):
                if t == 3:
                    upper(5)
                evac(GRP["v"] + t, v_[:, t])
            for t in range(NT):
                g = GRP["r"] + t
                act.wait_ge(proj, g + 1)
                if t >= 1:
                    act.wait_ge(rg_ready, t)
                else:
                    act.wait_ge(gla_kq, 6)
                act.activation(rg[:, t], ps[:, g % 4], ACT.Copy).then_inc(sig_r, 1)
                act.activation(tmpG[:, 0], ps[:, g % 4], ACT.Sigmoid).then_inc(proj_out, 1)

            def expo(u):
                act.wait_ge(m_ready, u + 1)
                n = (u // MH + 1) * P
                act.activation(Pm[:, u % 4, 0:n], Pm[:, u % 4, 0:n], ACT.Exp, bias=nmax[:, u:u + 1],
                               accum_out=rsum[:, u:u + 1]).then_inc(p_exp, 1)

            def pt_copy(u):
                act.wait_ge(pt_done, u + 1)
                if u >= 2:
                    act.wait_ge(pv_done, u - 1)
                n = (u // MH + 1) * P
                act.activation(PTs[:, u % 2, 0:n], ps[:, 6 + u % 2, 0:n], ACT.Copy).then_inc(pt_out, 1)

            def h_square(t):
                act.wait_ge(h_ready, 2 * t + 2)
                if t == 0:
                    act.wait_ge(y_zeroed, 16)
                else:
                    act.wait_ge(f_stored, 16 * t)
                    act.wait_ge(ft_done, 2 * t)
                act.activation(F, H[:, t], ACT.Square, accum_out=ss[:, 4:5]).then_inc(h_ss, 1)

            def store_f(t):
                act.wait_ge(f_ready, t + 1)
                act.dma_start(f_rows[t * P:(t + 1) * P, :], F).then_inc(f_stored, 16)

            for t in range(NT):
                for i in range(MH + 1):
                    if i < MH:
                        expo(t * MH + i)
                    if i >= 1:
                        pt_copy(t * MH + i - 1)
                    if i == 3:
                        act.wait_ge(go_done, t + 1)
                        if t >= 1:
                            act.wait_ge(tg_done, t)
                        act.activation(ON, ps[:, 1], ACT.Square).then_inc(go_sq, 1)
                    if t >= 1 and i == MH - 1:
                        h_square(t - 1)
                act.wait_ge(tg_done, t + 1)
                act.activation(actT[:, 4:8, t * P:(t + 1) * P], ps[:, 2].rearrange("p (c q) -> p c q", c=4), ACT.Copy,
                               scale=vc[:, 18:19]).then_inc(tg_out, 1)
                act.wait_ge(tm_done, t + 1)
                act.activation(actT[:, 0:4, t * P:(t + 1) * P], ps[:, 2].rearrange("p (c q) -> p c q", c=4), ACT.Copy).then_inc(tm_out, 1)
                if t >= 1:
                    store_f(t - 1)
            h_square(NT - 1)
            store_f(NT - 1)
            act.wait_ge(wo_done, 2 * NT)
            act.dma_start(wpp, w_ple_proj[0].rearrange("(c p) n -> p c n", p=P)).then_inc(ple_ld, 16)
            act.dma_start(prow, p[0, 0].rearrange("(t p) n -> p t n", p=P)).then_inc(ple_ld, 16)
            act.wait_ge(e_in, 1)
            act.activation(ex4[:], ex4[:], ACT.Exp).then_inc(e_out, 1)
            for i in range(2):
                act.dma_start(b12raw[i * NE:(i + 1) * NE, 0:2 * D], b1[0]).then_inc(bias_in, 16)
                act.dma_start(b12raw[i * NE:(i + 1) * NE, 2 * D:3 * D], b2[0]).then_inc(bias_in, 16)
            for c in range(2):
                act.wait_ge(pt2_done, c + 1)
                act.activation(pT[:, c], ps[:, 4 + c], ACT.Copy).then_inc(pt2_out, 1)
            for t in range(NT):
                a = 2 * (t % 2)
                pl = ps[:, a:a + 2].rearrange("p a n -> p (a n)")
                act.wait_ge(pp_done, t + 1)
                act.activation(pleo[:, t], pl, ACT.Square, accum_out=ss[:, 7:8]).then_inc(pp_ss, 1)
                act.wait_ge(pp_rs, t + 1)
                act.activation(pleo[:, t], pl, ACT.Copy, scale=rstd[:, 5:6]).then_inc(pp_out, 1)

            act.wait_ge(bias_in, 64)
            act.activation(BB[:], b12raw, ACT.Copy).then_inc(bb_hi, 1)

            def split_hi(b, p, first=False):
                q, k = p // RING, p % RING
                if k == 0:
                    act.wait_ge(w_in_s[q], b * 16 + 16)
                if not first:
                    act.wait_ge(piece_used, b * PIECES + (p + 1 - RING))
                act.activation(WS[:, k, 0], w1q[:, q, 2 * k:2 * k + 2], ACT.Copy).then_inc(w_hi, 1)

            def split_x(b):
                act.wait_ge(xt_ready, b * 2 + 2)
                act.activation(XTh[:], XTf, ACT.Copy).then_inc(xh_ready, 1)

            def sigmoid(b, q, first):
                act.wait_ge(glu_min, b * 4 + (q + 1))
                if q > 0 or not first:
                    act.wait_ge(hid_ready, b * 4 + q)
                act.activation(SIG, T1, ACT.Sigmoid, scale=ALPHA).then_inc(sig_done, 1)

            def hidden_out(b, g, first):
                act.wait_ge(th_done, b * 2 + (g + 1))
                if not first:
                    act.wait_ge(w2_used, b * 2 + (g - 1))
                act.activation(HIDT[:, 4 * g:4 * g + 4], ps[:, 6 + g, 0:4 * CAP].rearrange("p (f j) -> p f j", f=4),
                               ACT.Copy).then_inc(ht_out, 1)

            def store_y(b, first=False):
                act.wait_ge(y_done, b + 1)
                if not first:
                    act.wait_ge(y_stored, b * 16)
                for i in range(2):
                    act.activation(YR[:, i * 512:(i + 1) * 512], ps[0:CAP, 4 + i], ACT.Copy).then_inc(yr_out, 1)
                act.wait_ge(yr_out, b * 2 + 2)
                act.dma_start(y_rows[bass.ds(b * CAP, CAP), :], YR).then_inc(y_stored, 16)

            def expert_block(b, first=False, second=False):
                if not first:
                    for p in range(0, 4):
                        split_hi(b, p)
                    store_y(b - 1, second)
                for p in range(4, 9):
                    split_hi(b, p)
                sigmoid(b, 0, first)
                for p in range(9, 15):
                    split_hi(b, p)
                sigmoid(b, 1, first)
                for p in range(15, 16):
                    split_hi(b, p)
                sigmoid(b, 2, first)
                hidden_out(b, 0, first)
                sigmoid(b, 3, first)
                act.wait_ge(h1_done, b * 4 + 4)
                split_x(b + 1)
                hidden_out(b, 1, first)

            act.wait_ge(ple_stored, 16 * NT)
            split_hi(0, 0, True)
            split_x(0)
            for k in range(1, RING):
                split_hi(0, k, True)
            expert_block(0, True)
            expert_block(1, False, True)
            with act.Fori(2, NE) as b:
                expert_block(b)
            n = extra_blocks(act, lambda i: expert_block(i + NE))
            store_y(n + (NE - 1))
            act.wait_ge(y_stored, (n + NE) * 16)
            act.activation(held[:], tok[0:1, 0:1], ACT.Copy).then_inc(blocks_done, 1)
            def tail_norm(t):
                act.wait_ge(h3_ready, t + 1)
                if t >= 2:
                    act.wait_ge(o_stored[t % 2], 16 * (t // 2))
                act.activation(OUTB[:, t % 2], H[:, t], ACT.Square, accum_out=ssg[:, t:t + 1]).then_inc(h3_ss, 1)

            def h2_turned(t):
                for i in range(2):
                    act.wait_ge(h2t_done, 2 * t + i + 1)
                    act.activation(actT[:, 4 * i:4 * i + 4, t * P:(t + 1) * P], ps[:, i].rearrange("p (c q) -> p c q", c=4),
                                   ACT.Copy).then_inc(h2t_out, 1)

            h2_turned(0)
            for t in range(NT):
                if t >= 1:
                    tail_norm(t - 1)
                if t < NT - 1:
                    h2_turned(t + 1)
                act.wait_ge(gm_done, t + 1)
                if t >= 2:
                    act.wait_ge(h3_ready, t - 1)
                a = 2 + 2 * (t % 2)
                act.activation(SG[:, t % 2], ps[:, a:a + 2].rearrange("p a n -> p (a n)"), ACT.Sigmoid).then_inc(gm_sig, 1)
            tail_norm(NT - 1)

        @block.tensor
        def _(pe):
            pe.wait_ge(consts, 1)
            pe.wait_ge(vec_in, 80)
            pe.transpose(ps[:, 7, 0:19], vraw, ident[0:19, 0:19]).then_inc(turned, 1)
            for c in range(NC):
                if c >= 4:
                    pe.wait_ge(at_lo, c - 3)
                for t in range(NT):
                    if c == 0:
                        pe.wait_ge(xs_ready, t + 1)
                    last = pe.transpose(ps[:, c % 4, t * P:(t + 1) * P], xs[:, t, c * P:(c + 1) * P], ident[:])
                last.then_inc(proj, 1)
            def group(g, dst, pairs, inc=proj):
                pe.wait_ge(proj_out, g - 3)
                for i, (l, r) in enumerate(pairs):
                    last = pe.matmul(dst, l, r, start=(i == 0), stop=(i == len(pairs) - 1))
                last.then_inc(inc, 1)

            pe.wait_ge(small_in, 48)
            pe.wait_ge(at_lo, NC)
            pe.wait_ge(wag_lo, 1)
            group(GRP_AG, ps[0:RANK, GRP_AG % 4],
                  [pair_ for c in range(NC) for pair_ in ((wagh[:, c], aTh[:, c]), (wagh[:, c], aTl[:, c]), (wagl[:, c], aTh[:, c]))])
            pe.wait_ge(proj_out, GRP_AG + 1)
            for hp in range(2):
                g = GRP_GATE + hp
                group(g, ps[:, g % 4], [(wgate[:, hp * P:(hp + 1) * P], agT)])

            for i, (name, _) in enumerate(CH):
                if name == "v":
                    pe.wait_ge(kt_ready, 2)
                    for hp in range(2):
                        g = GRP["ktok"] + hp
                        pe.wait_ge(proj_out, g - 3)
                        for t in range(NT):
                            last = pe.transpose(ps[:, g % 4, t * P:(t + 1) * P], ktail[:, hp, t * P:(t + 1) * P], ident[:])
                        last.then_inc(proj, 1)
                    pe.wait_ge(proj_out, GRP["ktok"] + 2)
                    for c in range(7):
                        t, r = c // 2, GC * (c % 2)
                        bank, at = 4 + c % 2 + 2 * (t // 2), 256 * (t % 2)
                        for h in range(GH):
                            lo = 64 * (h % 2)
                            last = pe.matmul(ps[lo:lo + 64, bank, at + (h // 2) * P:at + (h // 2 + 1) * P],
                                             ktok[r:r + GC, t, h * 64:(h + 1) * 64], vg[r:r + GC, t, h * P:(h + 1) * P],
                                             start=True, stop=True)
                        last.then_inc(kv_done, 1)
                for j in range(4):
                    g = GRP[name] + j
                    pe.wait_ge(proj_out, g - 3)
                    for c in range(NC):
                        if j == 0 and c % 2 == 0:
                            pe.wait_ge(p_lo, 4 * i + c // 2 + 1)
                        if name in ("qk_g", "q", "k"):
                            cols = slice(j * P, (j + 1) * P)
                            pairs = [(PWh[:, c, cols], aTh[:, c]), (PWh[:, c, cols], aTl[:, c]), (PWl[:, c, cols], aTh[:, c])]
                        else:
                            rows = slice(j * P, (j + 1) * P)
                            pairs = [(aTh[:, c, rows], PWh[:, c]), (aTh[:, c, rows], PWl[:, c]), (aTl[:, c, rows], PWh[:, c])]
                        for m, (l, r) in enumerate(pairs):
                            last = pe.matmul(ps[:, g % 4], l, r, start=(c == 0 and m == 0), stop=(c == NC - 1 and m == 2))
                        if j == 3 and c in (1, 3, 5):
                            last.then_inc(p_used, 1)
                    last.then_inc(proj, 1)

            def mix_out(t, n, c):
                if c == 0:
                    pe.wait_ge(wst_in[n], (112, 16)[n])
                    pe.wait_ge(tm_out, t + 1)
                    pe.wait_ge(tg_out, t + 1)
                    if t >= 1 and n == 0:
                        pe.wait_ge(lg_out, t)
                    if 2 * t + n >= 1:
                        pe.wait_ge(h_ready, 2 * t + n)
                last = pe.matmul(ps[:, 3], actT[:, c, t * P:(t + 1) * P], wst[:, n, c], start=(c == 0), stop=(c == NC - 1))
                if c == NC - 1:
                    last.then_inc(wo_done, 1)

            def ffn_in(t):
                pe.wait_ge(f_ready, t + 1)
                for i in (1, 0):
                    if i == 0:
                        pe.wait_ge(om_out, min(t + 2, NT))
                    else:
                        pe.wait_ge(on_ready, min(t + 2, NT))
                    for c in range(4):
                        last = pe.transpose(ps[:, i, c * P:(c + 1) * P], F[:, (4 * i + c) * P:(4 * i + c + 1) * P], ident[:])
                    last.then_inc(ft_done, 1)

            def router(t):
                pe.wait_ge(ft_out, 2 * t + 2)
                for c in range(NC):
                    pe.matmul(ps[:, 3, 0:NE], actT[:, c, t * P:(t + 1) * P], wr[:, c], start=(c == 0), stop=False)
                pe.matmul(ps[:, 3, 0:NE], ones[0:1, :], brow[:], start=False, stop=True).then_inc(lg_done, 1)

            pe.wait_ge(proj_out, NGRP)
            pe.wait_ge(gla_kq, 6)
            pe.wait_ge(consts, 17)
            MIX_STEPS = [range(0, 2), range(2, 5), range(5, 8), range(8, 11), range(11, 14), range(14, 16)] + 4 * [range(0)]
            for t in range(NT):
                tt = slice(t * P, (t + 1) * P)
                if t >= 1:
                    pe.wait_ge(on_ready, t)
                if t >= 2:
                    pe.wait_ge(ft_out, 2 * t - 2)
                for h in range(GH):
                    last = pe.matmul(ps[:, 1, h * P:(h + 1) * P], kd[:, h // 2, tt], qz[:, h, tt], start=True, stop=True)
                last.then_inc(a_done, 1)
                for i in range(MH + 2):
                    if i < MH:
                        u, lo = t * MH + i, 64 * (i % 2)
                        if u >= 2:
                            pe.wait_ge(s_masked, u - 1)
                        else:
                            pe.wait_ge(st_ready, 14)
                        pe.matmul(ps[:, 4 + i % 2, 0:(t + 1) * P], qT[lo:lo + 64, i // 2, tt], kT[lo:lo + 64, i // 2, 0:(t + 1) * P],
                                  start=True, stop=True).then_inc(s_done, 1)
                    if t >= 1:
                        for c in MIX_STEPS[i]:
                            mix_out(t - 1, c // NC, c % NC)
                    if 1 <= i <= MH:
                        u = t * MH + i - 1
                        pe.wait_ge(p_exp, u + 1)
                        if u >= 2:
                            pe.wait_ge(pt_out, u - 1)
                        for k in range(t + 1):
                            last = pe.transpose(ps[:, 6 + u % 2, k * P:(k + 1) * P], Pm[:, u % 4, k * P:(k + 1) * P], ident[:])
                        last.then_inc(pt_done, 1)
                    if i >= 2:
                        h = i - 2
                        u = t * MH + h
                        pe.wait_ge(pt_out, u + 1)
                        if t >= 1 and h == 0:
                            pe.wait_ge(om_out, t)
                        for k in range(t + 1):
                            last = pe.matmul(ps[:, 0, h * 64:(h + 1) * 64], PTs[:, u % 2, k * P:(k + 1) * P], v_[:, k, h * 64:(h + 1) * 64],
                                             start=(k == 0), stop=(k == t))
                        last.then_inc(pv_done, 1)
                    if i == 2:
                        pe.wait_ge(a_out, t + 1)
                        for h in range(GH):
                            for e in range(2):
                                c = 2 * t + e
                                pe.matmul(ps[e * GC:(e + 1) * GC, 1, h * P:(h + 1) * P], qz[:, h, c * GC:(c + 1) * GC], st[:, c, h // 2],
                                          start=True, stop=False)
                            last = pe.matmul(ps[:, 1, h * P:(h + 1) * P], AT[:, h * P:(h + 1) * P], vg[:, t, h * P:(h + 1) * P],
                                             start=False, stop=True)
                        last.then_inc(go_done, 1)
                pe.wait_ge(on_ready, t + 1)
                if t >= 1:
                    pe.wait_ge(tm_out, t)
                for c in range(4):
                    last = pe.transpose(ps[:, 2, c * P:(c + 1) * P], ON[:, c * P:(c + 1) * P], ident[:])
                last.then_inc(tg_done, 1)
                if t >= 1:
                    ffn_in(t - 1)
                pe.wait_ge(om_out, t + 1)
                pe.wait_ge(tg_out, t + 1)
                for c in range(4):
                    last = pe.transpose(ps[:, 2, c * P:(c + 1) * P], OMS[:, c * P:(c + 1) * P], ident[:])
                last.then_inc(tm_done, 1)
                if t >= 1:
                    router(t - 1)
            for n in range(2):
                for c in range(NC):
                    mix_out(NT - 1, n, c)
            ffn_in(NT - 1)
            router(NT - 1)
            pe.wait_ge(ple_ld, 32)
            for c in range(2):
                for t in range(NT):
                    last = pe.transpose(ps[:, 4 + c, t * P:(t + 1) * P], prow[:, t, c * P:(c + 1) * P], ident[:])
                last.then_inc(pt2_done, 1)
            pe.wait_ge(mk_ready, 1)
            pe.matmul(ps[:, 7, 0:(NT + 1) * NE], ones[:], PX[:], start=True, stop=False)
            last = pe.matmul(ps[:, 7, 0:NT * NE], before[:], Mk[:], start=False, stop=True)
            last.then_inc(rank_done, 1)
            pe.wait_ge(pt2_out, 2)
            pe.wait_ge(lg_out, NT)

            def ple_tile(t):
                a = 2 * (t % 2)
                if t >= 2:
                    pe.wait_ge(pp_out, t - 1)
                for n in range(2):
                    for c in range(2):
                        last = pe.matmul(ps[:, a + n], pT[:, c, t * P:(t + 1) * P], wpp[:, c, n * 512:(n + 1) * 512],
                                         start=(c == 0), stop=(c == 1))
                last.then_inc(pp_done, 1)
            for t in range(NT - 1):
                ple_tile(t)
            pe.wait_ge(oh_ready, 1)
            for a in range(NT * TOPK):
                last = pe.matmul(ps[0:CAP, 4, 0:NTAB], ohJ[:, a, :], ohB[:, a, :], start=(a == 0), stop=(a == NT * TOPK - 1))
            last.then_inc(tok_done, 1)
            ple_tile(NT - 1)

            def turn_x(b):
                pe.wait_ge(xg_in, b * 16 + 16)
                for c in range(NC):
                    last = pe.transpose(ps[:, 6 + c // 4, (c % 4) * CAP:(c % 4 + 1) * CAP], XG[:, c * P:(c + 1) * P], ident[0:CAP, 0:CAP])
                last.then_inc(xt_done, 1)

            def hidden_quarter(b, q, first):
                for k in range(RING):
                    pe.wait_ge(w_lo, b * PIECES + (RING * q + k + 1))
                    if k == 0 and q == 0:
                        pe.wait_ge(xl_ready, b + 1)
                    if k == 0 and not first:
                        pe.wait_ge(hid_ready, b * 4 + (q - 3))
                    for cc in range(2):
                        c = 2 * k + cc
                        pe.matmul(ps[0:CAP, q], XTh[:, c], WS[:, k, 0, cc], start=(c == 0), stop=False)
                        pe.matmul(ps[0:CAP, q], XTh[:, c], WS[:, k, 1, cc], start=False, stop=False)
                        last = pe.matmul(ps[0:CAP, q], XTl[:, c], WS[:, k, 0, cc], start=False, stop=False)
                    last.then_inc(piece_used, 1)
                    if q == 3 and k == 2:
                        pe.wait_ge(xt_ready, b * 2 + 4)
                        turn_hidden(b, 0)
                if q == 0:
                    pe.wait_ge(sel_ready, b + 1)
                    if first:
                        pe.wait_ge(bb_ready, 1)
                pe.matmul(ps[0:CAP, q], sel[:], BB[:, q * 512:(q + 1) * 512], start=False, stop=True).then_inc(h1_done, 1)

            def turn_hidden(b, g):
                pe.wait_ge(hid_ready, b * 4 + (2 * g + 2))
                for f in range(4 * g, 4 * g + 4):
                    last = pe.transpose(ps[:, 6 + g, (f % 4) * CAP:(f % 4 + 1) * CAP], HIDr[:, f * P:(f + 1) * P], ident[0:CAP, 0:CAP])
                last.then_inc(th_done, 1)

            def expert_block(b, first):
                hidden_quarter(b, 0, first)
                turn_x(b + 1)
                hidden_quarter(b, 1, first)
                hidden_quarter(b, 2, first)
                hidden_quarter(b, 3, first)
                if not first:
                    pe.wait_ge(yr_out, b * 2)
                for f in range(NC):
                    if f == 3:
                        turn_hidden(b, 1)
                    if f % 4 == 0:
                        pe.wait_ge(w_in_s[4 + f // 4], b * 16 + 16)
                        pe.wait_ge(ht_out, b * 2 + (f // 4 + 1))
                    for n in range(2):
                        last = pe.matmul(ps[0:CAP, 4 + n], HIDT[:, f], w2h[:, f, n * 512:(n + 1) * 512], start=(f == 0), stop=False)
                    if f % 4 == 3:
                        last.then_inc(w2_used, 1)
                for n in range(2):
                    last = pe.matmul(ps[0:CAP, 4 + n], sel[:], BB[:, 2 * D + n * 512:2 * D + (n + 1) * 512], start=False, stop=True)
                last.then_inc(y_done, 1)

            pe.wait_ge(pp_out, NT)
            turn_x(0)
            expert_block(0, True)
            with pe.Fori(1, NE) as b:
                expert_block(b, False)
            extra_blocks(pe, lambda i: expert_block(i + NE, False))

            pe.wait_ge(wst_in[0], 128)
            pe.wait_ge(wst_in[1], 32)
            def turn_h2(t):
                pe.wait_ge(h2_ready, t + 1)
                for i in range(2):
                    if t >= 1:
                        pe.wait_ge(h2t_out, 2 * t - 1 + i)
                    for c in range(4):
                        last = pe.transpose(ps[:, i, c * P:(c + 1) * P], H[:, t, (4 * i + c) * P:(4 * i + c + 1) * P], ident[:])
                    last.then_inc(h2t_done, 1)

            turn_h2(0)
            for t in range(NT):
                pe.wait_ge(h2t_out, 2 * t + 2)
                if t >= 2:
                    pe.wait_ge(gm_sig, t - 1)
                for n in range(2):
                    for c in range(NC):
                        last = pe.matmul(ps[:, 2 + 2 * (t % 2) + n], actT[:, c, t * P:(t + 1) * P], wpg[:, n, c],
                                         start=(c == 0), stop=(c == NC - 1))
                    if n == 0 and t < NT - 1:
                        turn_h2(t + 1)
                last.then_inc(gm_done, 1)

        @block.vector
        def _(dve):
            made = [0]

            def link(ins):
                made[0] += 1
                ins.then_inc(dve_step, 1)
                dve.wait_ge(dve_step, made[0])

            def mean(i, src):
                return dve.tensor_scalar(ss[:, i:i + 1], src, 1.0 / D, EPS, ALU.mult, ALU.add)

            dve.wait_ge(turned, 1)
            dve.tensor_copy(vc[:], ps[:, 7, 0:19]).then_inc(turned_out, 1)
            dve.wait_ge(ms_ready, NT)
            dve.tensor_scalar(ss[:, 0:NT], ss[:, 0:NT], 1.0 / D, EPS, ALU.mult, ALU.add).then_inc(x_rstd, 1)
            dve.wait_ge(rstd_ready, 1)
            for t in range(NT):
                dve.tensor_scalar(xs[:, t], H[:, t], rstd[:, t:t + 1], None, ALU.mult).then_inc(xs_ready, 1)
            dve.wait_ge(consts, 1)
            dve.tensor_tensor(pair[:], ident[0:2 * NE, 0:NE], ident[0:2 * NE, NE:2 * NE], ALU.add).then_inc(pair_ready, 1)
            dve.memset(PX[:, 0], 0.0).then_inc(pair_ready, 1)
            for g in range(NC):
                dve.wait_ge(proj_out, g + 1)
                dve.scalar_tensor_tensor(out=aTl[:, g], in0=ps[:, g % 4], scalar=vc[:, g:g + 1], in1=aTh[:, g].bitcast(F32),
                                         op0=ALU.mult, op1=ALU.subtract).then_inc(at_lo, 1)
                if g == 4:
                    dve.wait_ge(wag_hi, 1)
                    dve.tensor_tensor(wagl[:], wag[:], wagh[:].bitcast(F32), ALU.subtract).then_inc(wag_lo, 1)

            def rest(i):
                for k in range(4):
                    c = slice(2 * k, 2 * k + 2)
                    dve.wait_ge(p_hi, 4 * i + k + 1)
                    dve.tensor_tensor(PWl[:, c], wst[:, 0, c], PWh[:, c].bitcast(F32), ALU.subtract).then_inc(p_lo, 1)

            rest(0)
            dve.wait_ge(gx_ready, 1)
            link(dve.tensor_scalar(G, G, 0.0, None, ALU.min))
            dve.wait_ge(gln, 1)
            link(dve.tensor_tensor(G, G, tmpG, ALU.subtract))
            dve.wait_ge(consts, 4)
            for hp in range(2):
                dve.tensor_tensor_scan(G[:, hp], keep, G[:, hp], 0.0, ALU.mult, ALU.add).then_inc(g_ready, 1)
            dve.wait_ge(g_ready, 2)
            for hp in range(2):
                gv = G[:, hp].rearrange("p (c s) -> p c s", s=GC)
                dve.tensor_tensor(ktail[:, hp].rearrange("p (c s) -> p c s", s=GC), gv[:, :, GC - 1:GC].to_broadcast([P, 8, GC]), gv,
                                  ALU.subtract).then_inc(dg_ready, 1)
            rest(1)
            dve.wait_ge(proj_out, GRP["qk_g"] + 4)
            dve.wait_ge(eg_ready, 1)
            for h in range(GH):
                lo = 64 * (h % 2)
                dve.tensor_tensor(qz[lo:lo + 64, h], qraw[lo:lo + 64, h // 2], eG[lo:lo + 64, h // 2], ALU.mult).then_inc(gla_kq, 1)
            dve.wait_ge(eg_neg, 1)
            for hp in range(2):
                dve.tensor_tensor(kd[:, hp], kraw[:, hp], tmpG[:, hp], ALU.mult).then_inc(gla_kq, 1)
            rest(2)
            dve.wait_ge(dg_exp, 1)
            for hp in range(2):
                dve.tensor_tensor(ktail[:, hp], ktail[:, hp], kraw[:, hp], ALU.mult).then_inc(kt_ready, 1)
            rest(3)
            rest(4)
            dve.wait_ge(consts, 16)
            dve.wait_ge(kv_done, 7)
            for c in range(7):
                bank, at = 4 + c % 2 + 2 * (c // 4), 256 * ((c // 2) % 2)
                if c >= 1:
                    dve.wait_ge(st_ready, 2 * c)
                for hp in range(2):
                    dve.scalar_tensor_tensor(out=st[:, c + 1, hp], in0=st[:, c, hp], scalar=eG[:, hp, c * GC + GC - 1:c * GC + GC],
                                             in1=ps[:, bank, at + hp * P:at + (hp + 1) * P], op0=ALU.mult, op1=ALU.add).then_inc(st_ready, 1)
            rest(5)
            for t in range(NT):
                dve.wait_ge(proj_out, GRP["r"] + t + 1)
                dve.wait_ge(sig_r, t + 1)
                dve.tensor_tensor(rg[:, t], rg[:, t], tmpG[:, 0], ALU.mult).then_inc(rg_ready, 1)

            def add_mix(t, n):
                dve.wait_ge(wo_done, 2 * t + n + 1)
                if t == 0:
                    dve.wait_ge(x_back, 16 * NT)
                dve.tensor_tensor(H[:, t, n * 512:(n + 1) * 512], H[:, t, n * 512:(n + 1) * 512], ps[:, 3], ALU.add).then_inc(h_ready, 1)

            def ffn_mean(t):
                dve.wait_ge(h_ss, t + 1)
                mean(4, ss[:, 4:5]).then_inc(h_ms, 1)

            def ffn_rows(t):
                dve.wait_ge(h_rs, t + 1)
                dve.tensor_scalar(F, H[:, t], rstd[:, 4:5], None, ALU.mult).then_inc(f_ready, 1)

            def ffn_turned(t):
                for i in (1, 0):
                    dve.wait_ge(ft_done, 2 * t + 2 - i)
                    dve.tensor_tensor(actT[:, 4 * i:4 * i + 4, t * P:(t + 1) * P], ps[:, i].rearrange("p (c q) -> p c q", c=4),
                                      vc[:, 8 + 4 * i:12 + 4 * i].unsqueeze(2).to_broadcast([P, 4, P]), ALU.mult).then_inc(ft_out, 1)
                dve.wait_ge(lg_done, t + 1)
                dve.tensor_copy(L[:, t], ps[:, 3, 0:NE]).then_inc(lg_out, 1)
                dve.wait_ge(lg_out, t + 1)
                link(dve.max(top8[:, t], L[:, t]))
                link(dve.max_index(idx8[:, t], top8[:, t], L[:, t]))

            dve.wait_ge(consts, 17)
            for t in range(NT):
                n = (t + 1) * P
                dve.wait_ge(a_done, t + 1)
                if t >= 1:
                    dve.wait_ge(go_done, t)
                dve.copy_predicated(AT, chunk_ok[:].rearrange("p h q -> p (h q)"), ps[:, 1]).then_inc(a_out, 1)
                for h in range(MH):
                    u = t * MH + h
                    dve.wait_ge(s_done, u + 1)
                    if u >= 4:
                        dve.wait_ge(pt_done, u - 3)
                    dve.scalar_tensor_tensor(out=Pm[:, u % 4, 0:n], in0=dist[:, dbase[t]:dbase[t] + n], scalar=slope[h],
                                             in1=ps[:, 4 + h % 2, 0:n], op0=ALU.mult, op1=ALU.add).then_inc(s_masked, 1)
                    dve.wait_ge(s_masked, u + 1)
                    dve.tensor_reduce(nmax[:, u:u + 1], Pm[:, u % 4, 0:n], AX.X, ALU.max, negate=True).then_inc(m_ready, 1)
                    if t >= 1 and h == 3:
                        add_mix(t - 1, 0)
                    if h == 4:
                        dve.wait_ge(go_sq, t + 1)
                        link(dve.tensor_reduce(ssg[:], ON.rearrange("p (h v) -> p h v", h=GH), AX.X, ALU.add))
                        dve.tensor_scalar(ssg[:], ssg[:], 1.0 / P, EPS, ALU.mult, ALU.add).then_inc(go_ss, 1)
                    if h == 5:
                        dve.wait_ge(go_rs, t + 1)
                        link(dve.tensor_tensor(ON.rearrange("p (h v) -> p h v", h=GH), ps[:, 1].rearrange("p (h v) -> p h v", h=GH),
                                               rsg[:].unsqueeze(2).to_broadcast([P, GH, P]), ALU.mult))
                        dve.wait_ge(rg_ready, NT)
                        dve.tensor_tensor(ON, ON, rg[:, t], ALU.mult).then_inc(on_ready, 1)
                    if t >= 1 and h == 6:
                        add_mix(t - 1, 1)
                if t >= 1:
                    ffn_mean(t - 1)
                dve.wait_ge(p_exp, (t + 1) * MH)
                link(dve.reciprocal(rinv[:, t * MH:(t + 1) * MH], rsum[:, t * MH:(t + 1) * MH]))
                if t >= 1:
                    ffn_rows(t - 1)
                dve.wait_ge(pv_done, (t + 1) * MH)
                if t >= 1:
                    dve.wait_ge(tm_done, t)
                dve.tensor_tensor(OMS.rearrange("p (h v) -> p h v", h=MH), ps[:, 0].rearrange("p (h v) -> p h v", h=MH),
                                  rinv[:, t * MH:(t + 1) * MH].unsqueeze(2).to_broadcast([P, MH, HD]), ALU.mult).then_inc(om_out, 1)
                if t >= 1:
                    ffn_turned(t - 1)
            add_mix(NT - 1, 0)
            add_mix(NT - 1, 1)
            ffn_mean(NT - 1)
            ffn_rows(NT - 1)
            ffn_turned(NT - 1)

            A = NT * TOPK
            link(dve.tensor_copy(idxf[:], idx8[:, :, 0:TOPK]))
            link(dve.tensor_tensor(oh, it_b[:, 0:NE].unsqueeze(1).to_broadcast([P, A, NE]),
                                   idxf[:].rearrange("p t k -> p (t k)").unsqueeze(2).to_broadcast([P, A, NE]), ALU.is_equal))
            dve.wait_ge(pair_ready, 2)
            link(dve.tensor_reduce(Mk[:], oh.rearrange("p (t k) e -> p t e k", k=TOPK), AX.X, ALU.add))
            for t in range(NT):
                ins = dve.tensor_tensor(PX[:, t + 1], PX[:, t], Mk[:, t], ALU.add)
                if t < NT - 1:
                    link(ins)
                else:
                    ins.then_inc(mk_ready, 1)
            dve.tensor_tensor(ex4[:], top8[:, :, 0:TOPK], top8[:, :, 0:1].to_broadcast([P, NT, TOPK]), ALU.subtract).then_inc(e_in, 1)
            dve.wait_ge(e_out, 1)
            link(dve.tensor_reduce(s4[:], ex4[:], AX.X, ALU.add))
            link(dve.reciprocal(s4[:], s4[:]))
            link(dve.tensor_tensor(gate[:], ex4[:], s4[:].unsqueeze(2).to_broadcast([P, NT, TOPK]), ALU.mult))
            dve.wait_ge(rank_done, 1)
            link(dve.tensor_copy(cnt[:], ps[:, 7, NT * NE:(NT + 1) * NE]))
            link(dve.tensor_scalar(extra[:], cnt[:], CAP + 0.5, None, ALU.is_gt))
            for j in range(2, MAXFULL + 1):
                link(dve.scalar_tensor_tensor(out=extra[:], in0=cnt[:], scalar=j * CAP + 0.5, in1=extra[:], op0=ALU.is_gt, op1=ALU.add))
            link(dve.tensor_tensor_scan(xend[:], ones[:, 0:NE], extra[:], 0.0, ALU.mult, ALU.add))
            link(dve.tensor_tensor(xbase[:], xend[:], extra[:], ALU.subtract))
            link(dve.tensor_tensor(xbase[:], xbase[:], it_b[:, 0:NE], ALU.subtract))
            rank = ps[:, 7, 0:NT * NE].rearrange("p (t e) -> p t e", t=NT)
            link(dve.tensor_copy(Jm, rank))
            link(dve.tensor_scalar(full, Jm, CAP - 0.5, None, ALU.is_gt))
            link(dve.tensor_copy(has, full))
            for j in range(2, MAXFULL + 1):
                link(dve.scalar_tensor_tensor(out=full, in0=Jm, scalar=j * CAP - 0.5, in1=full, op0=ALU.is_gt, op1=ALU.add))
            link(dve.scalar_tensor_tensor(out=Jm, in0=full, scalar=-float(CAP), in1=Jm, op0=ALU.mult, op1=ALU.add))
            link(dve.tensor_scalar(xbase[:], xbase[:], float(NE - 1), None, ALU.add))
            link(dve.tensor_tensor(has, has, xbase[:].unsqueeze(1).to_broadcast([P, NT, NE]), ALU.mult))
            link(dve.tensor_tensor(has, has, full, ALU.add))
            link(dve.tensor_tensor(has, has, it_b[:, 0:NE].unsqueeze(1).to_broadcast([P, NT, NE]), ALU.add))
            for src, dst in ((has, Bs), (Jm, Js)):
                for t in range(NT):
                    pr = dve.tensor_tensor(prod[:, t * TOPK:(t + 1) * TOPK], oh[:, t * TOPK:(t + 1) * TOPK],
                                           src[:, t:t + 1].to_broadcast([P, TOPK, NE]), ALU.mult)
                link(pr)
                link(dve.tensor_reduce(dst[:], prod, AX.X, ALU.add))
            link(dve.tensor_tensor(ohB, it_b[:].unsqueeze(1).to_broadcast([P, A, NTAB]), Bs[:].unsqueeze(2).to_broadcast([P, A, NTAB]), ALU.is_equal))
            for t in range(NT):
                tt = ohB[:, t * TOPK:(t + 1) * TOPK]
                link(dve.tensor_scalar(tt, tt, tok[:, t:t + 1], None, ALU.mult))
            dve.tensor_tensor(ohJ, it_j[:].unsqueeze(1).to_broadcast([P, A, CAP]), Js[:].unsqueeze(2).to_broadcast([P, A, CAP]),
                              ALU.is_equal).then_inc(oh_ready, 1)
            link(dve.scalar_tensor_tensor(out=slotf[:], in0=Bs[:], scalar=float(CAP), in1=Js[:], op0=ALU.mult, op1=ALU.add))
            link(dve.tensor_copy(sloti[:], slotf[:]))
            link(dve.tensor_tensor(xcmp, it_b[0:1, 0:NEXTRA].unsqueeze(2).to_broadcast([1, NEXTRA, NE]),
                                   xend[0:1, :].unsqueeze(1).to_broadcast([1, NEXTRA, NE]), ALU.is_ge))
            link(dve.tensor_reduce(tabf[:, 0:NEXTRA], xcmp, AX.X, ALU.add))
            link(dve.tensor_scalar(tabf[:, 0:NEXTRA], tabf[:, 0:NEXTRA], float(NE - 1), None, ALU.min))
            link(dve.tensor_copy(tabf[:, NEXTRA:NEXTRA + 1], xend[0:1, NE - 1:NE]))
            link(dve.tensor_copy(tab[:], tabf[:]))
            dve.wait_ge(tok_done, 1)
            dve.tensor_copy(tokix[:], ps[0:CAP, 4, 0:NTAB]).then_inc(tab_ready, 1)

            def turned_x(b):
                dve.wait_ge(xt_done, b + 1)
                for i in range(2):
                    dve.tensor_tensor(XTf[:, 4 * i:4 * i + 4], ps[:, 6 + i, 0:4 * CAP].rearrange("p (c j) -> p c j", c=4),
                                      vc[:, 8 + 4 * i:12 + 4 * i].unsqueeze(2).to_broadcast([P, 4, CAP]), ALU.mult).then_inc(xt_ready, 1)

            def rest_x(b):
                dve.wait_ge(xt_ready, b * 2 + 2)
                dve.wait_ge(xh_ready, b + 1)
                dve.tensor_tensor(XTl[:], XTf, XTh[:].bitcast(F32), ALU.subtract).then_inc(xl_ready, 1)

            def split_lo(b, p):
                q, k = p // RING, p % RING
                dve.wait_ge(w_hi, b * PIECES + (p + 1))
                dve.tensor_tensor(WS[:, k, 1], w1q[:, q, 2 * k:2 * k + 2], WS[:, k, 0].bitcast(F32), ALU.subtract).then_inc(w_lo, 1)

            def choose_bias(e):
                dve.tensor_tensor(sel[:], pair[:, bass.ds(e, 1)].to_broadcast([2 * NE, CAP]), ones[0:2 * NE, 0:CAP], ALU.mult).then_inc(sel_ready, 1)

            def swiglu(b, q, first):
                s0 = 2 * q
                dve.wait_ge(h1_done, b * 4 + (q + 1))
                if q > 0 or not first:
                    dve.wait_ge(hid_ready, b * 4 + q)
                dve.tensor_scalar(T1, ps[0:CAP, q, 0:512:2], LIMIT, None, ALU.min).then_inc(glu_min, 1)
                dve.tensor_scalar(T2, ps[0:CAP, q, 1:512:2], LIMIT, -LIMIT, ALU.min, ALU.max).then_inc(moe_step, 1)
                dve.wait_ge(moe_step, b * SWI + (s0 + 1))
                dve.wait_ge(glu_min, b * 4 + (q + 1))
                dve.scalar_tensor_tensor(out=T2, in0=T2, scalar=1.0, in1=T1, op0=ALU.add, op1=ALU.mult).then_inc(moe_step, 1)
                dve.wait_ge(moe_step, b * SWI + (s0 + 2))
                dve.wait_ge(sig_done, b * 4 + (q + 1))
                if not first:
                    dve.wait_ge(th_done, b * 2 + (q // 2 - 1))
                dve.tensor_tensor(HIDr[:, q * 256:(q + 1) * 256], T2, SIG, ALU.mult).then_inc(hid_ready, 1)

            def expert_block(b, e, first=False):
                if not first:
                    for p in range(0, 4):
                        split_lo(b, p)
                    dve.wait_ge(y_done, b)
                    choose_bias(e)
                for p in range(4, 8):
                    split_lo(b, p)
                dve.wait_ge(xl_ready, b + 1)
                turned_x(b + 1)
                for p in range(8, 9):
                    split_lo(b, p)
                swiglu(b, 0, first)
                for p in range(9, 15):
                    split_lo(b, p)
                swiglu(b, 1, first)
                for p in range(15, 16):
                    split_lo(b, p)
                swiglu(b, 2, first)
                swiglu(b, 3, first)
                rest_x(b + 1)

            turned_x(0)
            split_lo(0, 0)
            rest_x(0)
            for k in range(1, RING):
                split_lo(0, k)
            choose_bias(0)
            dve.wait_ge(bb_hi, 1)
            dve.tensor_tensor(BB[NE:2 * NE, :], b12raw[NE:2 * NE, :], BB[NE:2 * NE, :].bitcast(F32), ALU.subtract).then_inc(bb_ready, 1)
            expert_block(0, 0, True)
            with dve.Fori(1, NE) as b:
                expert_block(b, b)

            def body(i):
                e = dve.value_load(tab[0:1, bass.ds(i, 1)], min_val=0, max_val=NE - 1)
                expert_block(i + NE, e)
            extra_blocks(dve, body)

            def tail(t):
                dve.wait_ge(gm_sig, t + 1)
                dve.wait_ge(ple_scaled, t + 1)
                if t == 0:
                    dve.wait_ge(tail_in, 48)
                link(dve.tensor_tensor(SG[:, t % 2], SG[:, t % 2], ple_in[:, t], ALU.mult))
                dve.tensor_tensor(H[:, t], H[:, t], SG[:, t % 2], ALU.add).then_inc(h3_ready, 1)

            def last_norm(t):
                dve.wait_ge(h3_ss, t + 1)
                mean(6, ssg[:, t:t + 1]).then_inc(h3_ms, 1)
                dve.wait_ge(h3_rs, t + 1)
                dve.scalar_tensor_tensor(out=OUTB[:, t % 2], in0=H[:, t], scalar=rstd[:, 6:7], in1=gfin, op0=ALU.mult,
                                         op1=ALU.mult).then_inc(o_ready, 1)

            def add_experts(t):
                for k in range(TOPK):
                    dve.wait_ge(yg_in[t * TOPK + k], 16)
                    ins = dve.scalar_tensor_tensor(out=H[:, t], in0=yg[:, t * TOPK + k], scalar=gate[:, t, k:k + 1], in1=H[:, t],
                                                   op0=ALU.mult, op1=ALU.add)
                    if k < TOPK - 1:
                        link(ins)
                    else:
                        ins.then_inc(h2_ready, 1)

            add_experts(0)
            add_experts(1)
            for t in range(NT):
                if t < NT - 2:
                    add_experts(t + 2)
                tail(t)
                last_norm(t)



_INS = ['x', 'p', 'g_mix', 'w_in', 'w_gla_gate', 'b_gla_gate', 'g_gla_norm', 'w_out', 'g_ffn', 'w_router', 'b_router',
        'w1', 'b1', 'w2', 'b2', 'w_ple_gate', 'w_ple_proj', 'g_ple', 'g_final']
_OUTS = [((1, 512, 1024), 'float32')]


def kernel(**inputs):
    import numpy as _np
    import concourse.bacc as _bacc
    from concourse import mybir as _mybir
    from concourse.bass_utils import run_bass_kernel_spmd as _run

    nc = _bacc.Bacc("TRN2", target_bir_lowering=False, num_devices=1)
    arrays, args = {}, []
    for name in _INS:
        a = _np.ascontiguousarray(inputs[name])
        arrays[f"in_{name}_dram"] = a
        args.append(nc.dram_tensor(f"in_{name}_dram", a.shape, _mybir.dt.from_np(a.dtype), kind="ExternalInput").ap())
    for i, (shape, dtype) in enumerate(_OUTS):
        dt = _mybir.dt.from_np(_np.dtype(dtype))
        args.append(nc.dram_tensor(f"out_{i}_dram", shape, dt, kind="ExternalOutput").ap())
    hybrid_layer(nc, *args)
    r = _run(nc, [arrays], core_ids=[0])
    return r.results[0]["out_0_dram"]
```
